# Optimizing a Trainium2 kernel written in Bass

```python
import jax
import jax.numpy as jnp
from jax import lax
import numpy as np
import math
import jax, jax.numpy as jnp

D_MODEL = 1024
BATCH = 1
SEQ = 512
DEPTH = 1

N_MEM = 256
EPS = 1e-6
D_FF = 2816
HG_HEADS = 4
HG_DK = 128
HG_DV = 128
HG_CHUNK = 64
HG_K = HG_HEADS * HG_DK
HG_V = HG_HEADS * HG_DV
HG_COLS = 2 * HG_K + 2 * HG_V
DIL_GROUPS = ((128, 1), (512, 4), (2048, 16))
DIL_HEADS = 4
DIL_DH = 128
DIL_W = DIL_HEADS * DIL_DH
DIL_COLS = len(DIL_GROUPS) * 3 * DIL_W
ALIBI_HEADS = len(DIL_GROUPS) * DIL_HEADS
MEM_HEADS = 4
MEM_DH = 128
MEM_W = MEM_HEADS * MEM_DH
N_BRANCH = 3
GATE_COLS = N_BRANCH * D_MODEL
SPLITS = (HG_K, 2 * HG_K, 2 * HG_K + HG_V, HG_COLS, HG_COLS + DIL_COLS, HG_COLS + DIL_COLS + MEM_W)
D_IN = HG_COLS + DIL_COLS + MEM_W + GATE_COLS


def rmsnorm(x, w):
    xf = x.astype(jnp.float32)
    y = xf * lax.rsqrt(jnp.mean(xf * xf, axis=-1, keepdims=True) + EPS)
    return (y * w.astype(jnp.float32)).astype(x.dtype)

def swiglu(x, w_gu, w_down):
    g, u = jnp.split(x @ w_gu, 2, axis=-1)
    return (jax.nn.silu(g) * u) @ w_down

def alibi_slopes():
    return 2.0 ** (-8.0 * jnp.arange(1, ALIBI_HEADS + 1, dtype=jnp.float32) / ALIBI_HEADS)

def hgrn2(q_raw, f_raw, i_raw, lb):
    B, S = q_raw.shape[:2]
    C = HG_CHUNK
    N = S // C
    f32 = jnp.float32
    q = jax.nn.silu(q_raw.astype(f32)).reshape(B, N, C, HG_HEADS, HG_DK)
    lbh = lb.reshape(HG_HEADS, HG_DK)
    f = lbh + (1.0 - lbh) * jax.nn.sigmoid(f_raw.astype(f32).reshape(B, N, C, HG_HEADS, HG_DK))
    k = 1.0 - f
    v = i_raw.astype(f32).reshape(B, N, C, HG_HEADS, HG_DV)
    b = jnp.cumsum(jnp.log(f), axis=2)
    ref = b[:, :, C // 2 - 1:C // 2]
    scores = jnp.einsum('bnchk,bnshk->bnhcs', q * jnp.exp(b - ref), k * jnp.exp(ref - b))
    causal = jnp.tril(jnp.ones((C, C), dtype=bool))
    scores = jnp.where(causal, scores, 0.0)
    o_intra = jnp.einsum('bnhcs,bnshv->bnchv', scores, v)
    b_last = b[:, :, -1:]
    kv = jnp.einsum('bnshk,bnshv->nbhkv', k * jnp.exp(b_last - b), v)
    decay = jnp.moveaxis(jnp.exp(b_last[:, :, 0]), 1, 0)

    def step(state, inp):
        kv_n, dec_n = inp
        return dec_n[..., None] * state + kv_n, state

    s0 = jnp.zeros((B, HG_HEADS, HG_DK, HG_DV), f32)
    _, s_prev = lax.scan(step, s0, (kv, decay))
    o_inter = jnp.einsum('bnchk,nbhkv->bnchv', q * jnp.exp(b), s_prev)
    return (o_intra + o_inter).reshape(B, S, HG_HEADS, HG_DV)

def dilated_group(q, k, v, window, dil, slopes):
    B, S, H, dh = q.shape
    nk = window // dil
    span = nk * dil
    Sp = -(-S // span) * span
    L = Sp // dil
    nb = L // nk

    def to_sub(t):
        t = jnp.pad(t, ((0, 0), (0, Sp - S), (0, 0), (0, 0)))
        return t.reshape(B, L, dil, H, dh).transpose(0, 2, 1, 3, 4).reshape(B * dil, nb, nk, H, dh)

    qs, ks, vs = to_sub(q), to_sub(k), to_sub(v)
    kb = jnp.concatenate([jnp.pad(ks, ((0, 0), (1, 0), (0, 0), (0, 0), (0, 0)))[:, :-1], ks], axis=2)
    vb = jnp.concatenate([jnp.pad(vs, ((0, 0), (1, 0), (0, 0), (0, 0), (0, 0)))[:, :-1], vs], axis=2)
    s = jnp.einsum('znqhd,znkhd->znhqk', qs, kb).astype(jnp.float32) * (dh ** -0.5)
    qi = jnp.arange(nk)[:, None]
    kj = jnp.arange(2 * nk)[None, :]
    delta = nk + qi - kj
    blk = jnp.arange(nb)[:, None, None]
    valid = (delta >= 0) & (delta <= nk) & ((blk > 0) | (kj >= nk))
    s = s - slopes[:, None, None] * (delta * dil).astype(jnp.float32)
    s = jnp.where(valid[:, None], s, -jnp.inf)
    m = jnp.max(s, axis=-1)
    p = jnp.exp(s - m[..., None])
    l = jnp.sum(p, axis=-1)
    o = jnp.einsum('znhqk,znkhd->znqhd', p.astype(vb.dtype), vb).astype(jnp.float32)
    o = o.reshape(B, dil, L, H, dh).transpose(0, 2, 1, 3, 4).reshape(B, Sp, H, dh)[:, :S]

    def stat_back(t):
        return t.transpose(0, 1, 3, 2).reshape(B, dil, L, H).transpose(0, 2, 1, 3).reshape(B, Sp, H)[:, :S]

    return o, stat_back(m), stat_back(l)

def dilated_attention(dil_cols):
    B, S = dil_cols.shape[:2]
    qkv = dil_cols.reshape(B, S, len(DIL_GROUPS), 3, DIL_HEADS, DIL_DH)
    slopes = alibi_slopes()
    outs, maxs, sums = [], [], []
    for g, (window, dil) in enumerate(DIL_GROUPS):
        o, m, l = dilated_group(qkv[:, :, g, 0], qkv[:, :, g, 1], qkv[:, :, g, 2], window, dil,
                                slopes[g * DIL_HEADS:(g + 1) * DIL_HEADS])
        outs.append(o)
        maxs.append(m)
        sums.append(l)
    m_all = jnp.stack(maxs)
    w = jnp.exp(m_all - jnp.max(m_all, axis=0))
    num = jnp.sum(w[..., None] * jnp.stack(outs), axis=0)
    den = jnp.sum(w * jnp.stack(sums), axis=0)
    return (num / den[..., None]).reshape(B, S, DIL_W).astype(dil_cols.dtype)

def memory_attention(mq, mem, mem_norm_w, w_mem_kv):
    B, S = mq.shape[:2]
    mk, mv = jnp.split(rmsnorm(mem, mem_norm_w) @ w_mem_kv, 2, axis=-1)
    mq = mq.reshape(B, S, MEM_HEADS, MEM_DH)
    mk = mk.reshape(B, N_MEM, MEM_HEADS, MEM_DH)
    mv = mv.reshape(B, N_MEM, MEM_HEADS, MEM_DH)
    s = jnp.einsum('bshd,bmhd->bhsm', mq, mk).astype(jnp.float32) * (MEM_DH ** -0.5)
    p = jax.nn.softmax(s, axis=-1).astype(mv.dtype)
    return jnp.einsum('bhsm,bmhd->bshd', p, mv).reshape(B, S, MEM_W)

def token_mixing(u, mem, w_in, b_gate, lb, hg_norm_w, mem_norm_w, w_mem_kv, w_br_hg, w_br_dil, w_br_mem, w_out):
    B, S, D = u.shape
    proj = u @ w_in
    hq, hf, hi, hog, dcols, mq, gl = jnp.split(proj, SPLITS, axis=-1)
    o_hg = rmsnorm(hgrn2(hq, hf, hi, lb), hg_norm_w)
    o_hg = o_hg * jax.nn.sigmoid(hog.astype(jnp.float32)).reshape(B, S, HG_HEADS, HG_DV)
    y_hg = o_hg.reshape(B, S, HG_V).astype(u.dtype)
    y_dil = dilated_attention(dcols)
    y_mem = memory_attention(mq, mem, mem_norm_w, w_mem_kv)
    gates = jax.nn.sigmoid((gl + b_gate).astype(jnp.float32)).astype(u.dtype).reshape(B, S, N_BRANCH, D)
    y = (gates[:, :, 0] * (y_hg @ w_br_hg)
         + gates[:, :, 1] * (y_dil @ w_br_dil)
         + gates[:, :, 2] * (y_mem @ w_br_mem))
    return y @ w_out

def first_inputs(seed: int = 0) -> dict:
    key = jax.random.key(seed)
    ks = jax.random.split(key, 22)
    f32 = jnp.float32

    def w(k, shape, fan_in):
        return jax.random.normal(k, shape, f32) * (fan_in ** -0.5)

    def gain(k, n):
        return 1.0 + 0.05 * jax.random.normal(k, (DEPTH, n), f32)

    return {
        'x': jax.random.normal(ks[0], (BATCH, SEQ, D_MODEL), f32),
        'mem': jax.random.normal(ks[1], (BATCH, N_MEM, D_MODEL), f32),
        'ffn1_pre_w': gain(ks[2], D_MODEL),
        'ffn1_w_gu': w(ks[3], (DEPTH, D_MODEL, 2 * D_FF), D_MODEL),
        'ffn1_w_down': w(ks[4], (DEPTH, D_FF, D_MODEL), D_FF),
        'ffn1_post_w': gain(ks[5], D_MODEL),
        'mix_pre_w': gain(ks[6], D_MODEL),
        'w_in': w(ks[7], (DEPTH, D_MODEL, D_IN), D_MODEL),
        'b_gate': 0.01 * jax.random.normal(ks[8], (DEPTH, GATE_COLS), f32),
        'hg_lb_logits': 0.1 * jax.random.normal(ks[9], (DEPTH + 1, HG_K), f32),
        'hg_norm_w': gain(ks[10], HG_DV),
        'mem_norm_w': gain(ks[11], D_MODEL),
        'w_mem_kv': w(ks[12], (DEPTH, D_MODEL, 2 * MEM_W), D_MODEL),
        'w_br_hg': w(ks[13], (DEPTH, HG_V, D_MODEL), HG_V),
        'w_br_dil': w(ks[14], (DEPTH, DIL_W, D_MODEL), DIL_W),
        'w_br_mem': w(ks[15], (DEPTH, MEM_W, D_MODEL), MEM_W),
        'w_out': w(ks[16], (DEPTH, D_MODEL, D_MODEL), D_MODEL),
        'mix_post_w': gain(ks[17], D_MODEL),
        'ffn2_pre_w': gain(ks[18], D_MODEL),
        'ffn2_w_gu': w(ks[19], (DEPTH, D_MODEL, 2 * D_FF), D_MODEL),
        'ffn2_w_down': w(ks[20], (DEPTH, D_FF, D_MODEL), D_FF),
        'ffn2_post_w': gain(ks[21], D_MODEL),
    }

def first_block(x, mem, ffn1_pre_w, ffn1_w_gu, ffn1_w_down, ffn1_post_w, mix_pre_w, w_in, b_gate,
              hg_lb_logits, hg_norm_w, mem_norm_w, w_mem_kv, w_br_hg, w_br_dil, w_br_mem, w_out,
              mix_post_w, ffn2_pre_w, ffn2_w_gu, ffn2_w_down, ffn2_post_w):
    lb_all = jnp.cumsum(jax.nn.softmax(hg_lb_logits.astype(jnp.float32), axis=0), axis=0)
    h = x
    for l in range(DEPTH):
        h = h + 0.5 * rmsnorm(swiglu(rmsnorm(h, ffn1_pre_w[l]), ffn1_w_gu[l], ffn1_w_down[l]), ffn1_post_w[l])
        u = rmsnorm(h, mix_pre_w[l])
        y = token_mixing(u, mem, w_in[l], b_gate[l], lb_all[l], hg_norm_w[l], mem_norm_w[l], w_mem_kv[l],
                         w_br_hg[l], w_br_dil[l], w_br_mem[l], w_out[l])
        h = h + rmsnorm(y, mix_post_w[l])
        h = h + 0.5 * rmsnorm(swiglu(rmsnorm(h, ffn2_pre_w[l]), ffn2_w_gu[l], ffn2_w_down[l]), ffn2_post_w[l])
    return h


GRID_W = 64
CTX_LEN = 256
BLK = 128
WINDOW = 128
ROPE_BASE = 10000.0
NEG = -1e30

A_HEADS = 8
A_KV = 2
A_DH = 64
B_GROUPS = 4
B_DG = 64
B_CHUNK = 128
C_HEADS = 4
C_DQ = 32
C_DV = 64

D_MIX = A_HEADS * A_DH + B_GROUPS * B_DG + C_HEADS * C_DV
OFF_AQ = 0
OFF_AK = OFF_AQ + A_HEADS * A_DH
OFF_AV = OFF_AK + A_KV * A_DH
OFF_BU = OFF_AV + A_KV * A_DH
OFF_BV = OFF_BU + B_GROUPS * B_DG
OFF_CQ = OFF_BV + B_GROUPS * B_DG
OFF_CK = OFF_CQ + C_HEADS * 2 * C_DQ
OFF_CV = OFF_CK + C_HEADS * 2 * C_DQ
D_IN_2 = OFF_CV + C_HEADS * C_DV

MOE_GROUPS = 4
MOE_PER_GROUP = 4
N_EXPERTS = MOE_GROUPS * MOE_PER_GROUP
MOE_TOPK = 2
D_EXPERT = 512


def rmsnorm_2(x, g):
    xf = x.astype(jnp.float32)
    y = xf * lax.rsqrt(jnp.mean(xf * xf, axis=-1, keepdims=True) + EPS)
    return (y * g.astype(jnp.float32)).astype(x.dtype)

def axial_rope(x, rows, cols):
    dh = x.shape[-1]
    n = dh // 4
    inv = ROPE_BASE ** (-jnp.arange(n, dtype=jnp.float32) / n)
    xf = x.astype(jnp.float32)

    def rot(xp, pos):
        ang = pos[:, None] * inv
        cs = jnp.cos(ang)[None, :, None, :]
        sn = jnp.sin(ang)[None, :, None, :]
        x1, x2 = xp[..., :n], xp[..., n:]
        return jnp.concatenate([x1 * cs - x2 * sn, x1 * sn + x2 * cs], axis=-1)

    out = jnp.concatenate([rot(xf[..., :2 * n], rows), rot(xf[..., 2 * n:], cols)], axis=-1)
    return out.astype(x.dtype)

def _sink_probs(scores, sink):
    m = sink
    for s in scores:
        m = jnp.maximum(m, jnp.max(s, axis=-1, keepdims=True))
    es = [jnp.exp(s - m) for s in scores]
    den = jnp.exp(sink - m)
    for e in es:
        den = den + jnp.sum(e, axis=-1, keepdims=True)
    return [e / den for e in es]

def window_sink_attn(q, k, v, kc, vc, sink):
    Bn, S, Hq, dh = q.shape
    Hkv = k.shape[2]
    G = Hq // Hkv
    nb = S // BLK
    scale = dh ** -0.5
    qb = q.reshape(Bn, nb, BLK, Hkv, G, dh)

    def band(t):
        tp = jnp.pad(t, ((0, 0), (BLK, BLK), (0, 0), (0, 0))).reshape(Bn, nb + 2, BLK, Hkv, dh)
        return jnp.concatenate([tp[:, :-2], tp[:, 1:-1], tp[:, 2:]], axis=2)

    kb, vb = band(k), band(v)
    s_loc = jnp.einsum('bnqhgd,bnkhd->bnhgqk', qb, kb).astype(jnp.float32) * scale
    bi = jnp.arange(nb)[:, None, None]
    qpos = bi * BLK + jnp.arange(BLK)[None, :, None]
    kpos = (bi - 1) * BLK + jnp.arange(3 * BLK)[None, None, :]
    mask = (jnp.abs(kpos - qpos) <= WINDOW) & (kpos >= 0) & (kpos < S)
    s_loc = jnp.where(mask[None, :, None, None], s_loc, NEG)
    s_ctx = jnp.einsum('bnqhgd,bchd->bnhgqc', qb, kc).astype(jnp.float32) * scale
    p_loc, p_ctx = _sink_probs([s_loc, s_ctx], sink.astype(jnp.float32).reshape(Hkv, G, 1, 1))
    o = (jnp.einsum('bnhgqk,bnkhd->bnqhgd', p_loc.astype(v.dtype), vb)
         + jnp.einsum('bnhgqc,bchd->bnqhgd', p_ctx.astype(v.dtype), vc))
    return o.reshape(Bn, S, Hq * dh)

def ctx_sink_attn(qc, kc, vc, sink):
    Bn, L, Hq, dh = qc.shape
    Hkv = kc.shape[2]
    G = Hq // Hkv
    qg = qc.reshape(Bn, L, Hkv, G, dh)
    s = jnp.einsum('bqhgd,bkhd->bhgqk', qg, kc).astype(jnp.float32) * dh ** -0.5
    (p,) = _sink_probs([s], sink.astype(jnp.float32).reshape(Hkv, G, 1, 1))
    o = jnp.einsum('bhgqk,bkhd->bqhgd', p.astype(vc.dtype), vc)
    return o.reshape(Bn, L, Hq * dh)

def chunk_gmlp(u, v, ws, bs, gtok):
    Bn, L, _ = u.shape
    nc = L // B_CHUNK
    u = jax.nn.gelu(u).reshape(Bn, nc, B_CHUNK, B_GROUPS, B_DG)
    vf = jax.nn.gelu(v).astype(jnp.float32).reshape(Bn, nc, B_CHUNK, B_GROUPS, B_DG)
    mu = jnp.mean(vf, axis=-1, keepdims=True)
    var = jnp.mean(jnp.square(vf - mu), axis=-1, keepdims=True)
    vn = ((vf - mu) * lax.rsqrt(var + EPS) * gtok.astype(jnp.float32)).astype(u.dtype)
    s = jnp.einsum('gpq,bnqgd->bnpgd', ws, vn) + bs.T[:, :, None]
    return (u * s).reshape(Bn, L, B_GROUPS * B_DG)

def _diff_core(q1, q2, k1, k2, v, lam):
    scale = C_DQ ** -0.5
    p1 = jax.nn.softmax(jnp.einsum('bqhd,bkhd->bhqk', q1, k1).astype(jnp.float32) * scale, axis=-1)
    p2 = jax.nn.softmax(jnp.einsum('bqhd,bkhd->bhqk', q2, k2).astype(jnp.float32) * scale, axis=-1)
    w = p1 - lam * p2
    return jnp.einsum('bhqk,bkhe->bqhe', w.astype(v.dtype), v)

def diff_attn(q1, q2, k1, k2, v, lam):
    Bn, Lq, H, dq = q1.shape
    nb = Lq // BLK
    qb1 = q1.reshape(Bn, nb, BLK, H, dq).swapaxes(0, 1)
    qb2 = q2.reshape(Bn, nb, BLK, H, dq).swapaxes(0, 1)
    out = lax.map(lambda qs: _diff_core(qs[0], qs[1], k1, k2, v, lam), (qb1, qb2))
    return out.swapaxes(0, 1).reshape(Bn, Lq, H, v.shape[-1])

def diff_out(o, gsub, lam_init):
    Bn, L, H, dv = o.shape
    return (rmsnorm_2(o, gsub) * (1.0 - lam_init)).reshape(Bn, L, H * dv)

def token_mixers(h, hc, w_in, w_out, sink, ws, bs, gtok, gsub, lam, lam_init, rows, cols, ctx_out):
    Bn, S, _ = h.shape
    Lc = hc.shape[1]
    p = h @ w_in

    def heads(lo, hi, n, d):
        return p[..., lo:hi].reshape(Bn, S, n, d)

    def cproj(lo, hi, n, d):
        return (hc @ w_in[:, lo:hi]).reshape(Bn, Lc, n, d)

    qa = axial_rope(heads(OFF_AQ, OFF_AK, A_HEADS, A_DH), rows, cols)
    ka = axial_rope(heads(OFF_AK, OFF_AV, A_KV, A_DH), rows, cols)
    va = heads(OFF_AV, OFF_BU, A_KV, A_DH)
    ka_c = cproj(OFF_AK, OFF_AV, A_KV, A_DH)
    va_c = cproj(OFF_AV, OFF_BU, A_KV, A_DH)
    ya = window_sink_attn(qa, ka, va, ka_c, va_c, sink)
    yb = chunk_gmlp(p[..., OFF_BU:OFF_BV], p[..., OFF_BV:OFF_CQ], ws, bs, gtok)
    qd = axial_rope(heads(OFF_CQ, OFF_CK, 2 * C_HEADS, C_DQ), rows, cols).reshape(Bn, S, C_HEADS, 2, C_DQ)
    kd = axial_rope(heads(OFF_CK, OFF_CV, 2 * C_HEADS, C_DQ), rows, cols).reshape(Bn, S, C_HEADS, 2, C_DQ)
    vd = heads(OFF_CV, D_IN_2, C_HEADS, C_DV)
    kd_c = cproj(OFF_CK, OFF_CV, 2 * C_HEADS, C_DQ).reshape(Bn, Lc, C_HEADS, 2, C_DQ)
    vd_c = cproj(OFF_CV, D_IN_2, C_HEADS, C_DV)
    k1 = jnp.concatenate([kd_c[..., 0, :], kd[..., 0, :]], axis=1)
    k2 = jnp.concatenate([kd_c[..., 1, :], kd[..., 1, :]], axis=1)
    vall = jnp.concatenate([vd_c, vd], axis=1)
    yc = diff_out(diff_attn(qd[..., 0, :], qd[..., 1, :], k1, k2, vall, lam), gsub, lam_init)
    y = jnp.concatenate([ya, yb, yc], axis=-1) @ w_out
    if not ctx_out:
        return y, None
    ya_c = ctx_sink_attn(cproj(OFF_AQ, OFF_AK, A_HEADS, A_DH), ka_c, va_c, sink)
    yb_c = chunk_gmlp(hc @ w_in[:, OFF_BU:OFF_BV], hc @ w_in[:, OFF_BV:OFF_CQ], ws, bs, gtok)
    qd_c = cproj(OFF_CQ, OFF_CK, 2 * C_HEADS, C_DQ).reshape(Bn, Lc, C_HEADS, 2, C_DQ)
    yc_c = diff_out(diff_attn(qd_c[..., 0, :], qd_c[..., 1, :], kd_c[..., 0, :], kd_c[..., 1, :], vd_c, lam), gsub, lam_init)
    y_c = jnp.concatenate([ya_c, yb_c, yc_c], axis=-1) @ w_out
    return y, y_c

def hier_moe(h, w_rg, b_rg, w_re, b_re, w_gate, w_up, w_down):
    Bn, L, D = h.shape
    t = h.reshape(-1, D)
    pg = jax.nn.softmax((t @ w_rg).astype(jnp.float32) + b_rg.astype(jnp.float32), axis=-1)
    ptop, gsel = lax.top_k(pg, 1)
    le = ((t @ w_re).astype(jnp.float32) + b_re.astype(jnp.float32)).reshape(-1, MOE_GROUPS, MOE_PER_GROUP)
    le_g = jnp.sum(le * jax.nn.one_hot(gsel[:, 0], MOE_GROUPS, dtype=jnp.float32)[:, :, None], axis=1)
    lv, li = lax.top_k(le_g, MOE_TOPK)
    w = jax.nn.softmax(lv, axis=-1) * ptop
    eid = gsel * MOE_PER_GROUP + li
    gates = jnp.sum(jax.nn.one_hot(eid, N_EXPERTS, dtype=jnp.float32) * w[..., None], axis=1)
    y = jnp.zeros(t.shape, jnp.float32)
    for e in range(N_EXPERTS):
        he = jax.nn.silu(t @ w_gate[e]) * (t @ w_up[e])
        y = y + gates[:, e:e + 1] * (he @ w_down[e]).astype(jnp.float32)
    return y.astype(h.dtype).reshape(Bn, L, D)

def second_inputs(seed: int = 0) -> dict:
    key = jax.random.key(seed)
    ks = jax.random.split(key, 32)

    def nrm(k, shape, s):
        return jax.random.normal(k, shape, jnp.float32) * s

    D = D_MODEL
    return {
        'x': nrm(ks[0], (BATCH, SEQ, D), 1.0),
        'c': nrm(ks[1], (BATCH, D), 1.0),
        'ctx': nrm(ks[2], (BATCH, CTX_LEN, D), 1.0),
        'c_ctx': nrm(ks[3], (D,), 1.0),
        'w_ada': nrm(ks[4], (DEPTH, D, 6 * D), 0.2 * D ** -0.5),
        'b_ada': nrm(ks[5], (DEPTH, 6 * D), 0.01),
        'g_mix': 1.0 + nrm(ks[6], (DEPTH, D), 0.01),
        'w_in': nrm(ks[7], (DEPTH, D, D_IN_2), D ** -0.5),
        'sink': nrm(ks[8], (DEPTH, A_HEADS), 0.5),
        'ws_tok': nrm(ks[9], (DEPTH, B_GROUPS, B_CHUNK, B_CHUNK), B_CHUNK ** -0.5),
        'bs_tok': 1.0 + nrm(ks[10], (DEPTH, B_GROUPS, B_CHUNK), 0.02),
        'g_tok': 1.0 + nrm(ks[11], (DEPTH, B_GROUPS, B_DG), 0.01),
        'lam_q1': nrm(ks[12], (DEPTH, C_DQ), 0.1),
        'lam_k1': nrm(ks[13], (DEPTH, C_DQ), 0.1),
        'lam_q2': nrm(ks[14], (DEPTH, C_DQ), 0.1),
        'lam_k2': nrm(ks[15], (DEPTH, C_DQ), 0.1),
        'g_sub': 1.0 + nrm(ks[16], (DEPTH, C_DV), 0.01),
        'w_out': nrm(ks[17], (DEPTH, D_MIX, D), D_MIX ** -0.5),
        'g_ffn': 1.0 + nrm(ks[18], (DEPTH, D), 0.01),
        'w_rg': nrm(ks[19], (DEPTH, D, MOE_GROUPS), D ** -0.5),
        'b_rg': nrm(ks[20], (DEPTH, MOE_GROUPS), 0.01),
        'w_re': nrm(ks[21], (DEPTH, D, N_EXPERTS), D ** -0.5),
        'b_re': nrm(ks[22], (DEPTH, N_EXPERTS), 0.01),
        'w_gate': nrm(ks[23], (DEPTH, N_EXPERTS, D, D_EXPERT), D ** -0.5),
        'w_up': nrm(ks[24], (DEPTH, N_EXPERTS, D, D_EXPERT), D ** -0.5),
        'w_down': nrm(ks[25], (DEPTH, N_EXPERTS, D_EXPERT, D), D_EXPERT ** -0.5),
        'g_final': 1.0 + nrm(ks[26], (D,), 0.01),
    }

def second_block(x, c, ctx, c_ctx, w_ada, b_ada, g_mix, w_in, sink, ws_tok, bs_tok, g_tok,
              lam_q1, lam_k1, lam_q2, lam_k2, g_sub, w_out, g_ffn, w_rg, b_rg, w_re, b_re,
              w_gate, w_up, w_down, g_final):
    S = x.shape[1]
    ROWS = S // GRID_W
    rows = jnp.repeat(jnp.arange(ROWS, dtype=jnp.float32), GRID_W)
    cols = jnp.broadcast_to(jnp.arange(GRID_W, dtype=jnp.float32)[None, :], (ROWS, GRID_W)).reshape(-1)
    xc = ctx
    for l in range(DEPTH):
        last = l == DEPTH - 1
        mod = jax.nn.silu(c) @ w_ada[l] + b_ada[l]
        modc = jax.nn.silu(c_ctx) @ w_ada[l] + b_ada[l]
        sh1, sc1, gt1, sh2, sc2, gt2 = jnp.split(mod[:, None, :], 6, axis=-1)
        csh1, csc1, cgt1, csh2, csc2, cgt2 = jnp.split(modc[None, None, :], 6, axis=-1)
        lam_init = 0.8 - 0.6 * math.exp(-0.3 * l)
        lam = (jnp.exp(jnp.sum(lam_q1[l].astype(jnp.float32) * lam_k1[l].astype(jnp.float32)))
               - jnp.exp(jnp.sum(lam_q2[l].astype(jnp.float32) * lam_k2[l].astype(jnp.float32))) + lam_init)
        h = rmsnorm_2(x, g_mix[l]) * (1.0 + sc1) + sh1
        hc = rmsnorm_2(xc, g_mix[l]) * (1.0 + csc1) + csh1
        y, y_c = token_mixers(h, hc, w_in[l], w_out[l], sink[l], ws_tok[l], bs_tok[l], g_tok[l],
                              g_sub[l], lam, lam_init, rows, cols, not last)
        x = x + gt1 * y
        h2 = rmsnorm_2(x, g_ffn[l]) * (1.0 + sc2) + sh2
        x = x + gt2 * hier_moe(h2, w_rg[l], b_rg[l], w_re[l], b_re[l], w_gate[l], w_up[l], w_down[l])
        if not last:
            xc = xc + cgt1 * y_c
            hc2 = rmsnorm_2(xc, g_ffn[l]) * (1.0 + csc2) + csh2
            xc = xc + cgt2 * hier_moe(hc2, w_rg[l], b_rg[l], w_re[l], b_re[l], w_gate[l], w_up[l], w_down[l])
    return rmsnorm_2(x, g_final)


def setup_inputs(seed=0):
    out = dict(first_inputs(seed))
    for name, value in second_inputs(seed + 1).items():
        if name != "x":
            out[name + "_2"] = value
    return out


def reference(
    x, mem, ffn1_pre_w, ffn1_w_gu, ffn1_w_down, ffn1_post_w, mix_pre_w, w_in, b_gate,
    hg_lb_logits, hg_norm_w, mem_norm_w, w_mem_kv, w_br_hg, w_br_dil, w_br_mem, w_out,
    mix_post_w, ffn2_pre_w, ffn2_w_gu, ffn2_w_down, ffn2_post_w, c_2, ctx_2, c_ctx_2, w_ada_2,
    b_ada_2, g_mix_2, w_in_2, sink_2, ws_tok_2, bs_tok_2, g_tok_2, lam_q1_2, lam_k1_2, lam_q2_2,
    lam_k2_2, g_sub_2, w_out_2, g_ffn_2, w_rg_2, b_rg_2, w_re_2, b_re_2, w_gate_2, w_up_2,
    w_down_2, g_final_2,
):
    x = first_block(
        x, mem, ffn1_pre_w, ffn1_w_gu, ffn1_w_down, ffn1_post_w, mix_pre_w, w_in, b_gate,
        hg_lb_logits, hg_norm_w, mem_norm_w, w_mem_kv, w_br_hg, w_br_dil, w_br_mem, w_out,
        mix_post_w, ffn2_pre_w, ffn2_w_gu, ffn2_w_down, ffn2_post_w,
    )
    return second_block(
        x, c_2, ctx_2, c_ctx_2, w_ada_2, b_ada_2, g_mix_2, w_in_2, sink_2, ws_tok_2, bs_tok_2,
        g_tok_2, lam_q1_2, lam_k1_2, lam_q2_2, lam_k2_2, g_sub_2, w_out_2, g_ffn_2, w_rg_2,
        b_rg_2, w_re_2, b_re_2, w_gate_2, w_up_2, w_down_2, g_final_2,
    )


_drawn_inputs = setup_inputs


def setup_inputs(seed=0):
    import zlib

    import numpy as np

    out = dict(_drawn_inputs(seed))
    spreads = {}
    factors = {'b_gate': 8.0,
     'hg_lb_logits': 7.463,
     'mem_norm_w': 6.465,
     'ffn2_post_w': 3.461,
     'ctx_2': 6.175,
     'c_ctx_2': 6.473,
     'b_ada_2': 8.0,
     'g_mix_2': 8.0,
     'sink_2': 8.0,
     'bs_tok_2': 8.0,
     'g_tok_2': 8.0,
     'lam_q1_2': 8.0,
     'lam_k1_2': 8.0,
     'lam_q2_2': 8.0,
     'lam_k2_2': 8.0,
     'g_sub_2': 64.0,
     'g_ffn_2': 8.0,
     'w_rg_2': 3.215,
     'b_rg_2': 64.0,
     'w_re_2': 3.678,
     'b_re_2': 36.339,
     'w_gate_2': 2.991,
     'w_up_2': 2.795,
     'w_down_2': 2.792,
     'g_final_2': 30.364}
    for name, (base, spread) in spreads.items():
        noise = np.random.default_rng([zlib.crc32(name.encode()), seed]).standard_normal(out[name].shape)
        drawn = base * np.exp(spread * noise) if base else spread * noise
        out[name] = jnp.asarray(drawn.astype(out[name].dtype))
    for name, factor in factors.items():
        out[name] = (out[name] * factor).astype(out[name].dtype)
    return out
```

```python
import math
from contextlib import ExitStack

import numpy as np

import concourse.bass as bass
from concourse import mybir

F32 = mybir.dt.float32
U32 = mybir.dt.uint32
I32 = mybir.dt.int32
F32R = mybir.dt.float32r
ACT = mybir.ActivationFunctionType
ALU = mybir.AluOpType
AX = mybir.AxisListType.X

P = 128
SEQ, D = 512, 1024
KC = D // P
N_MEM = N_CTX = 256
D_FF = 2816
NF = D_FF // P
EPS = 1e-6
HEADS = 4
N_EXP, D_EXP = 16, 512
LAM_INIT = 0.8 - 0.6 * math.exp(0.0)
SLOTS = 4
SPLIT_SLOTS = 2
GROUP = 4
BIG = 4096.0
EARLY = 5

B_GU1 = 0
B_DN1 = B_GU1 + 2 * NF
B_MIX1 = B_DN1 + NF
N_MIX1 = 3 * HEADS + HEADS * (4 + 9) + 3 * 12 + 8
B_GU2 = B_MIX1 + N_MIX1
B_ADA_REST = B_GU2 + 4 * NF
B_DN2 = B_ADA_REST + 4
N_ADA_CTX = 16
B_MIX2 = B_DN2 + NF
N_MIX2 = 16 + 8
B_MOE = B_MIX2 + N_MIX2
N_BLOCKS = B_MOE + 12 * N_EXP
assert N_BLOCKS % SLOTS == 0

COLS = {}
_at = 0
for _name, _n in (("ffn1_pre", 8), ("ffn1_post", 8), ("mix_pre", 8), ("mix_post", 8), ("ffn2_pre", 8), ("ffn2_post", 8),
                  ("mem_norm", 8), ("g_mix", 8), ("g_ffn", 8), ("g_final", 8), ("b_gate", 24), ("b_ada", 48),
                  ("hg_lb0", 4), ("hg_lb1", 4), ("hg_norm", 1), ("g_sub", 1), ("sink", 8), ("lam", 4),
                  ("b_router", 20)):
    COLS[_name] = (_at, _at + _n)
    _at += _n
N_COLS = _at

CONSTS = {}
_at = 0
for _name, _n in (("ident", P), ("mean_d", P), ("ones", P), ("mean_128", P), ("mean_64", P), ("swap16", P),
                  ("swap8", P), ("before", P), ("slot", P), ("window", 384), ("first", 16)):
    CONSTS[_name] = (_at, _at + _n)
    _at += _n
N_CONSTS = _at


VALUE_KINDS = ("hg_v", "dil_v", "a_v", "c_v", "b_v")


class Tile:

    def __init__(self, kind, head, q, index, s0, n_soft, width, group, last):
        self.kind, self.head, self.q, self.index, self.s0, self.n_soft = kind, head, q, index, s0, n_soft
        self.width, self.group, self.last = width, group, last
        self.n_keys = width // P


def plan():
    tiles, pieces, groups, turns = [], [0], [0], []
    softs = [0]

    def add_tile(kind, head, q, width, last, n_soft=1):
        tiles.append(Tile(kind, head, q, len(tiles), softs[0], n_soft, width, groups[0], last))
        softs[0] += n_soft
        groups[0] += last
        return tiles[-1].index

    class Mixer:
        def __init__(self, block):
            self.steps, self.pending, self.soon, self.block = [], [], [], block

        def piece(self, kind, args, take, done=True):
            self.steps.append(("piece", pieces[0], self.block, kind, args, done))
            pieces[0] += 1
            if done:
                self.block += 1
            self.flush()
            if kind in VALUE_KINDS:
                self.soon.append(("turn", len(turns), pieces[0] - 1, kind, args))
                turns.append((kind, args))
            for _ in range(take):
                self.pop()

        def flush(self):
            self.steps += self.soon
            self.soon = []

        def rotate(self, *which):
            self.soon.append(("rope",) + which)

        def pop(self):
            self.flush()
            if self.pending:
                self.steps.append(self.pending.pop(0)[1])

        def finish(self, tag):
            while any(t == tag for t, _ in self.pending):
                self.pop()

        def later(self, tag, *step):
            self.pending.append((tag, step))

        def run(self, tag, ids, n, lead, tail):
            for k in range(lead, n + (2 if tail else 0)):
                self.later(tag, "attn", *(ids[k - d] if 0 <= k - d < len(ids) else None for d in (2, 1, 0)))

    m = Mixer(B_MIX1)
    ids = []
    for h in range(HEADS):
        for kind in ("mem_k", "mem_v", "mem_q"):
            m.piece(kind, (h,), 1)
        ids += [add_tile("mem", h, q, 256, q == 3) for q in range(4)]
        m.run("mem", ids, 4 * h + 4, 4 * h, h == HEADS - 1)
    for h in range(HEADS):
        m.finish("hg")
        for kind in ("hg_f", "hg_q", "hg_v", "hg_og"):
            m.piece(kind, (h,), 2 if len(m.pending) > 5 else 1)
        for stage in ("hg_front", "hg_scores", "hg_kv", "hg_out", "hg_norm"):
            m.later("hg", stage, h)
        for g in range(3):
            for kind in ("dil_q", "dil_k"):
                if g == 0 and kind == "dil_q":
                    m.finish("dil_qk")
                m.piece(kind, (h, g), 2 if len(m.pending) > 5 else 1)
        m.finish("dil")
        for g in range(3):
            m.piece("dil_v", (h, g), 2 if len(m.pending) > 5 else 1)
        ids = [add_tile("dil", h, q, 768, q == 3) for q in range(4)]
        m.run("dil_qk", ids, 4, 0, False)
        for k in (4, 5):
            m.later("dil", "attn", ids[k - 2], ids[3] if k == 4 else None, None)
    for b in ("mem", "hg", "dil"):
        m.finish({"mem": "mem", "hg": "hg", "dil": "dil"}[b])
        for n in range(0, KC, 2):
            for k in (0, 1):
                m.piece("gate", (b, n + k), 2 if len(m.pending) > 5 else 1)
            for k in (0, 1):
                m.piece("branch", (b, n + k), 0, done=k == 1)
    assert not m.pending
    for n in range(KC):
        m.piece("w_out", (n,), 0)
    assert m.block == B_GU2
    mix1 = m.steps

    m = Mixer(B_MIX2)
    m.piece("a_k", ("x",), 0, done=False)
    m.piece("a_k", ("c",), 0)
    m.rotate("ka", 0)
    m.piece("a_v", ("x",), 1, done=False)
    m.piece("a_v", ("c",), 0)
    for j in range(4):
        m.piece("a_q", (j,), 1)
        m.rotate("qa", j)
        ids = []
        for par in range(2):
            ids += [add_tile("a", 2 * j + par, q, (512 if q in (0, 3) else 640), par == 1 and q == 3) for q in range(4)]
        m.run("a", ids, 8, 0, True)
    assert softs[0] % 2 == 0
    for c in range(2):
        m.piece("c_k", (c, "x"), 1, done=False)
        m.piece("c_k", (c, "c"), 1)
        m.rotate("kc", c)
    for c in range(2):
        m.piece("c_q", (c,), 2)
        m.rotate("qc", c)
    for c in range(2):
        m.piece("c_v", (c, "x"), 2, done=False)
        m.piece("c_v", (c, "c"), 2)
    for c in range(2):
        m.piece("b_v", (c,), 3)
    m.later("b", "gmlp_norm")
    for c in range(2):
        m.piece("b_u", (c,), 3)
        m.later("b", "gmlp", c)
    for tag in ("a", "b"):
        m.finish(tag)
    for c in range(2):
        ids = [add_tile("c", 2 * c + par, q, 768, par == 1 and q == 3, 2) for par in range(2) for q in range(4)]
        m.run("c", ids, 8, 0, True)
        m.later("c", "diff_norm", c)
    m.finish("c")
    for n in range(KC):
        m.piece("w_out2", (n,), 0)
    assert m.block == B_MOE and not m.soon
    return mix1, m.steps, tiles, softs[0]


MIX1, MIX2, TILES, N_SOFT = plan()
SOFT_TILE = [t for t in TILES for _ in range(t.n_soft)]


def wide_before(t):
    return sum(1 for x in TILES[:t] if x.n_keys > 4)


def scaled_before(s):
    return sum(1 for k in range(s) if not (SOFT_TILE[k].kind == "c" and (k - SOFT_TILE[k].s0) == 1))


def copied_before(s):
    return sum(1 for x in SOFT_TILE[:s] if x.kind in ("dil", "a"))


def paired_before(t):
    return sum(1 for x in TILES[:t] if x.kind == "c")


SPLIT = [True] * N_BLOCKS
for _st in MIX1 + MIX2:
    if _st[0] == "piece" and _st[3] in ("mem_k", "mem_v", "branch", "w_out", "w_out2"):
        SPLIT[_st[2]] = False
for _f in range(NF):
    SPLIT[B_GU2 + 4 * _f] = SPLIT[B_GU2 + 4 * _f + 2] = None
for _b in range(B_ADA_REST, B_DN2):
    SPLIT[_b] = None
for _b in range(B_MOE, N_BLOCKS):
    SPLIT[_b] = False


def index_of(b):
    return sum(1 for x in SPLIT[:b] if x == SPLIT[b])


def slope(group, head):
    return 2.0 ** (-8.0 * (group * HEADS + head + 1) / (3 * HEADS))


def local_keys(q):
    lo, hi = max(q - 1, 0) * P, min(q + 2, 4) * P
    return lo, hi - lo


def two_blocks_kernel(nc, stream, x_t, mem_t, ctx_t, c_rows_d, cols_d, consts_d, tables_d, hgmask_d, dist_d, rope_d, gtok_d,
                      bs_d, ws_d, router_d, out):
    with ExitStack() as ctx:
        def sb(name, shape, dt=F32):
            return ctx.enter_context(nc.sbuf_tensor(name, shape, dt))

        def sem(name):
            return ctx.enter_context(nc.semaphore(name))

        ring = sb("ring", [P, SLOTS, 1024])
        w_hi, w_lo = sb("w_hi", [P, SPLIT_SLOTS, 1024], F32R), sb("w_lo", [P, SPLIT_SLOTS, 1024], F32R)
        h = sb("h", [P, KC, SEQ])
        u_hi, u_lo = sb("u_hi", [P, KC, SEQ], F32R), sb("u_lo", [P, KC, SEQ], F32R)
        cols = sb("cols", [P, N_COLS])
        consts = sb("consts", [P, N_CONSTS])
        sq = sb("sq", [P, 2, SEQ])
        rms = sb("rms", [P, SEQ])
        rinv = sb("rinv", [P, SEQ])
        tmp = sb("tmp", [P, 2, SEQ])
        hidden_t = sb("hidden_t", [P, 2, SEQ])
        yb = sb("yb", [P, 12, SEQ])
        small = sb("small", [P, 256])
        zero = sb("zero", [P, 2])
        rounds_i = sb("rounds_i", [P, 1], I32)
        hgmask = sb("hgmask", [P, SEQ], U32)

        AREA = 90 * 256

        def phase(*tensors):
            with ExitStack() as own:
                return [own.enter_context(nc.sbuf_tensor(name, shape, dt)) for name, shape, dt in tensors]

        (area,) = phase(("area", [P, AREA], F32))
        act_hi, act_lo = phase(("act_hi", [P, NF * SEQ], F32R), ("act_lo", [P, NF * SEQ], F32R))
        ctx_hi, ctx_lo = phase(("ctx_hi", [P, KC, N_CTX], F32R), ("ctx_lo", [P, KC, N_CTX], F32R))
        sel, sel_t, y_hi, y_lo = phase(("sel", [P, GROUP, 4, P], F32R), ("sel_t", [P, GROUP, SEQ], F32R),
                                       ("y_hi", [P, D], F32R), ("y_lo", [P, D], F32R))
        ps = ctx.enter_context(nc.psum_tensor("ps", [P, 8, SEQ], F32))

        def col(name, k=0, n=1):
            a = COLS[name][0] + k
            return cols[:, a:a + n]

        def const(name, lo=0, n=None):
            a, b = CONSTS[name]
            return consts[:, a + lo:(b if n is None else a + lo + n)]

        ident = const("ident")

        def region(start_kb, shape):
            n = int(np.prod(shape))
            v = area[:, start_kb * 256:start_kb * 256 + n]
            assert start_kb * 256 + n <= AREA
            if len(shape) == 2:
                v = v.rearrange("p (a b) -> p a b", b=shape[1])
            if len(shape) == 3:
                v = v.rearrange("p (a b c) -> p a b c", b=shape[1], c=shape[2])
            return v

        def ysb(n):
            return yb[:, (8 + n) % 12, :]

        silu_g = tmp
        mem_raw = yb[:, 4:8, :].rearrange("p a b -> p (a b)").rearrange("p (k t) -> p k t", t=N_MEM)
        mem_n = mem_raw
        mq = region(58, [HEADS, SEQ])
        mk = region(66, [HEADS, N_MEM])
        mv = region(70, [HEADS, 2, P])
        y_mix = region(58, [KC, SEQ])
        hg_sg, hg_k, hg_b, hg_t, hg_t2, hg_q, hg_v, hg_og, hg_qe, hg_sc = (region(2 * i, [SEQ]) for i in range(10))
        hg_ke, hg_kl, hg_qb = hg_t, hg_t2, hg_b
        hg_klt = region(2, [4, P])
        hg_state = region(20, [7, P])
        scan_keep = region(54, [SEQ])
        v_raw = hidden_t
        w_out_y = region(24, [KC, SEQ])
        dq = region(24, [3, SEQ])
        dk = region(30, [3, SEQ])
        dv = region(36, [3, 4, P])
        dist = region(42, [4, 768])
        sc = region(75, [768])
        pr = region(78, [2, 768])
        pt = region(84, [2, 768])
        ctx_raw = mem_raw
        rope = region(16, [4, SEQ])
        qa = region(24, [4, SEQ])
        ka = region(32, [768])
        va = region(35, [6, P])
        qc = region(38, [2, SEQ])
        kc = region(42, [2, 768])
        vc = region(48, [6, 256])
        ub = region(54, [2, SEQ])
        vf = region(58, [4, 256])
        vn = region(62, [4, 256])
        gtok = region(66, [256])
        bsb = region(67, [2, P])
        wst = region(68, [4, P])
        raw = region(70, [2, SEQ])
        router_w = region(74, [KC, 20])
        rot = sq[:, 1, :]
        u = region(24, [KC, SEQ])
        xe = region(40, [KC, SEQ])
        he = region(56, [SEQ])
        he_t = region(58, [4, P])
        logits_t = region(56, [SEQ])[0:20, :]
        moe_silu = region(60, [SEQ])
        rt = region(62, [4 * 100])
        gates_e = region(64, [N_EXP, 4])
        place = region(65, [N_EXP + GROUP, 4])
        routed = region(66, [4, N_EXP])
        gsel = region(67, [GROUP])
        t_hi = u_hi[:].rearrange("p k t -> p (k t)").rearrange("p (a b) -> p a b", b=D)
        t_lo = u_lo[:].rearrange("p k t -> p (k t)").rearrange("p (a b) -> p a b", b=D)

        omlb, lb, lam_neg = small[:, 0:4], small[:, 4:8], small[:, 8:9]
        lam_p, lam_e = small[:, 10:12], small[:, 12:14]
        c_rows = yb[:, 0:4, :].rearrange("p a b -> p (a b)").rearrange("p (c k) -> p c k", c=2)
        ada_prod = yb[:, 8:12, :].rearrange("p a b -> p (a b)").rearrange("p (c k) -> p c k", c=2)
        mod = small[:, 32:128]
        mod_v = mod.rearrange("p (n c) -> p n c", c=2)
        gain = small[:, 128:152]
        mx, negm, es, den, rden, dec = (small[:, 152 + 2 * i:154 + 2 * i] for i in range(6))
        hg_dec = small[:, 168:176]
        eps_col, lbt = small[:, 176:177], small[:, 180:192]
        gm_mean, gm_var, gm_r = small[:, 192:208], small[:, 208:224], small[:, 224:240]

        landed = [sem(f"landed{i}") for i in range(SLOTS)]
        names = """raw_used split_used split_done half_mm params tables1 tables2 mem_in ctx_in sq_done sum_done root_done
            inv_done normed chunk_made high_made h_done hidden_made hi_made split_hi absorbed place_shifted dve_link act_link silu_done act_done down_mm y_moved c_in c_silu ada_x ada_ctx x_summed ctx_summed prep_act
            prep_pe prep_dve piece_out qk_mm copied shift_done exp_done rden_done scaled paired transposed pt_act pt_dve
            pv_mm o_out turned_mm turned hg_f_done hg_ln_done hg_shifted hg_exps hg_keys hg_queries hg_turned hg_klt_done
            hg_score_mm hg_scored hg_kv_mm hg_states hg_out_mm hg_squares hg_mean hg_root hg_done branch_added
            swap_mm roped diff_sq diff_mean diff_root diff_done gelu_norm_in gelu_root gelu_normed gmlp_mm gmlp_done
            x_res logits_mm logits_out route_mm route_exp_in route_e2_in route_exp route_done place_mm count_mm rounds_known u_hi_done u_turned u_split
            sel_done sel_used xe_mm xe_out selt_mm selt_out gsel_mm gsel_out silu_e he_done he_turned he_moved down_e
            y_hi_done y_lo_done back_mm back_added stored""".split()
        S = {n: sem(n) for n in names}
        block = ctx.enter_context(nc.Block())

        N_NORM_U = {0: 8, 1: 16, 3: 24, 5: 32, 7: 40, 8: 48, 9: 56, 10: 64}
        N_H = {2: 8, 4: 16, 6: 24}

        def bank(i, lo=0, n=SEQ):
            return ps[:, i, lo:lo + n]

        def bank7_free(step):
            name, value = BANK7_READ[step]
            return S[name], value

        def piece_done(step):
            _, p, b, _, _, done = step
            if not done:
                return S["half_mm"], half_count(p)
            return S["split_used" if SPLIT[b] else "raw_used"], index_of(b) + 1

        @block.sync
        def _(sp):
            sp.dma_start(cols[:], cols_d).then_inc(S["params"], 16)
            sp.dma_start(consts[:], consts_d).then_inc(S["params"], 16)
            sp.dma_start(mem_raw, mem_t).then_inc(S["params"], 16)
            sp.dma_start(h[:], x_t).then_inc(S["params"], 16)
            sp.dma_start(hgmask[:], hgmask_d).then_inc(S["params"], 16)

            def load(b, turns=0, raw_step=0, split_step=0, index=None):
                if b >= SLOTS:
                    last = b - SLOTS
                    if SPLIT[last]:
                        sp.wait_ge(S["split_done"], index_of(last) + 1 + split_step * turns)
                    elif SPLIT[last] is None:
                        sp.wait_ge(S["ada_x"], index_of(last) + 1 + raw_step * turns)
                    else:
                        sp.wait_ge(S["raw_used"], index_of(last) + 1 + raw_step * turns)
                src = stream[b] if index is None else stream[bass.ds(index, 1)].rearrange("n p f -> (n p) f")
                sp.dma_start(ring[:, b % SLOTS, :], src).then_inc(landed[b % SLOTS], 16)

            def load_range(lo, hi, raw_step, split_step):
                for b in range(lo, min(lo + SLOTS, hi)):
                    load(b)
                n = (hi - lo) // SLOTS - 1
                with sp.Fori(0, n) as i:
                    for b in range(lo + SLOTS, lo + 2 * SLOTS):
                        load(b, i, raw_step, split_step, b + SLOTS * i)
                for b in range(lo + SLOTS * (n + 1), hi):
                    load(b)

            load_range(0, B_MIX1, 0, SLOTS)
            sp.wait_ge(S["down_mm"], 8)
            sp.dma_start(dist, dist_d).then_inc(S["tables1"], 16)
            sp.dma_start(scan_keep, tables_d).then_inc(S["tables1"], 16)
            for b in range(B_MIX1, B_GU2):
                load(b)
            sp.wait_ge(S["branch_added"], 3 * KC)
            sp.dma_start(c_rows, c_rows_d).then_inc(S["c_in"], 16)
            sp.dma_start(ctx_raw, ctx_t).then_inc(S["ctx_in"], 16)
            load_range(B_GU2, B_ADA_REST, 2, 2)
            for b in range(B_ADA_REST, B_DN2):
                load(b)
            load_range(B_DN2, B_MIX2, 0, SLOTS)
            sp.wait_ge(S["down_mm"], 16)
            sp.dma_start(rope, rope_d).then_inc(S["tables2"], 16)
            sp.dma_start(gtok, gtok_d).then_inc(S["tables2"], 16)
            sp.dma_start(bsb, bs_d).then_inc(S["tables2"], 16)
            sp.dma_start(wst, ws_d).then_inc(S["tables2"], 16)
            sp.dma_start(router_w, router_d).then_inc(S["tables2"], 16)
            for b in range(B_MIX2, B_MOE):
                load(b)
            rounds = sp.alloc_register("rounds")
            sp.reg_mov(rounds, 1)
            with sp.Fori(0, rounds) as r:
                with sp.Fori(0, N_EXP // GROUP) as g:
                    for j in range(12 * GROUP):
                        sp.wait_ge(S["raw_used"], index_of(B_MOE) + 1 - SLOTS + j + 192 * r + 48 * g)
                        sp.dma_start(ring[:, j % SLOTS, :],
                                     stream[bass.ds(B_MOE + 48 * g + j, 1)].rearrange("n p f -> (n p) f")
                                     ).then_inc(landed[j % SLOTS], 16)
                sp.wait_ge(S["rounds_known"], 1)
                sp.reg_load(rounds, rounds_i[0:1, 0:1])
            for k in range(KC):
                sp.wait_ge(S["normed"], N_NORM_U[9] + k + 1)
                sp.dma_start(out[:, k, :], u[:, k, :]).then_inc(S["stored"], 16)
            sp.wait_ge(S["stored"], 16 * KC)

        @block.tensor
        def _(pe):
            mm = nc.tensor.matmul

            def raw_block(b, turns=0, step=0):
                pe.wait_ge(landed[b % SLOTS], 16 * (b // SLOTS + 1) + (16 * step // SLOTS) * turns)
                return b % SLOTS

            def split_block(b, turns=0, step=0):
                pe.wait_ge(S["split_done"], index_of(b) + 1 + step * turns)
                return index_of(b) % SPLIT_SLOTS

            def tile_of(slot, k):
                return ring[:, slot, k * P:(k + 1) * P]

            def mm3(o, slot, k, x_hi, x_lo, start, stop):
                tile = slice(k * P, (k + 1) * P)
                mm(o, w_hi[:, slot, tile], x_hi, start=start, stop=False)
                mm(o, w_hi[:, slot, tile], x_lo, start=False, stop=False)
                return mm(o, w_lo[:, slot, tile], x_hi, start=False, stop=stop)

            def sums(m, bk, n, before=()):
                for s, v in before:
                    pe.wait_ge(s, v)
                for k in range(KC):
                    sum_chunk(m, k, bk, n)

            def sum_chunk(m, k, bk, n):
                pe.wait_ge(S["sq_done"], KC * m + k + 1)
                mm(bank(bk, 0, n), const("mean_d"), sq[:, k % 2, 0:n], start=k == 0,
                   stop=k == KC - 1).then_inc(S["sum_done"], 1)

            def gate_up(j, f, q, b, turns=0, step=0, first=False):
                pe.wait_ge(S["act_done"], NF * j + f + 1)
                for w in range(2):
                    slot = split_block(b + (w if j == 0 else 2 * w + 1), turns, step)
                    for k in range(KC):
                        if first:
                            pe.wait_ge(S["normed"], N_NORM_U[{0: 1, 1: 5}[j]] - KC + k + 1)
                        last = mm3(bank(2 * q + w), slot, k, u_hi[:, k, :], u_lo[:, k, :], k == 0, k == KC - 1)
                    last.then_inc(S["split_used"], 1)

            def down(kt, b, turns=0, first=False, final=False):
                slot = split_block(b, turns, 4)
                cols_kt = bass.ds(kt * SEQ, SEQ)
                for n in range(KC):
                    last = mm3(bank(n), slot, n, act_hi[:, cols_kt], act_lo[:, cols_kt], first, final)
                    if final:
                        last.then_inc(S["down_mm"], 1)
                if not final:
                    last.then_inc(S["split_used"], 1)

            def ffn_down(j, b0):
                pe.wait_ge(S["act_done"], 2 + NF * (j + 1))
                pe.wait_ge(S["root_done"], {0: 2, 1: 6}[j])
                down(0, b0, first=True)
                with pe.Fori(0, 5) as i:
                    for s in range(4):
                        down(4 * i + 1 + s, b0 + 1 + s, i)
                down(NF - 1, b0 + NF - 1, final=True)
                pe.wait_ge(S["down_mm"], KC * (j + 1))
                pe.sem_inc(S["split_used"], 1)

            pe.wait_ge(S["params"], 80)
            pe.wait_ge(S["prep_dve"], 1)
            mm(bank(6, 0, 2), const("ones")[0:32, :], lam_p[0:32, :], start=True, stop=True).then_inc(S["prep_pe"], 1)
            sums(0, 7, N_MEM)
            sums(1, 5, SEQ)

            for f in range(2):
                gate_up(0, f, f, B_GU1 + 2 * f, first=f == 0)
            with pe.Fori(0, 10) as i:
                for s in range(2):
                    gate_up(0, 2 * i + 2 + s, s, B_GU1 + 4 + 2 * s, i, 4)
            ffn_down(0, B_DN1)
            sums(2, 0, SEQ, [(S["y_moved"], 1)])
            sums(3, 7, SEQ, [(S["y_moved"], 8)])

            def piece(step):
                _, p, b, kind, args, done = step
                if p >= 2:
                    pe.wait_ge(S["piece_out"], p - 1)
                if p == 0:
                    pe.wait_ge(S["root_done"], 4)
                slot = split_block(b) if SPLIT[b] else raw_block(b)
                bk = p % 2
                if kind == "mem_v":
                    for t in range(2):
                        for k in range(KC):
                            last = mm(bank(bk, t * P, P), mem_n[:, k, t * P:(t + 1) * P], tile_of(slot, k),
                                      start=k == 0, stop=k == KC - 1)
                elif kind == "branch":
                    src = {"mem": 8, "hg": 0, "dil": 4}[args[0]]
                    half = args[1] % 2
                    if args[1] == 0:
                        if args[0] == "hg":
                            pe.wait_ge(S["hg_done"], HEADS)
                        else:
                            pe.wait_ge(S["o_out"], {"mem": HEADS, "dil": 2 * HEADS}[args[0]])
                    for k in range(4):
                        last = mm(bank(bk), tile_of(slot, 4 * half + k), yb[:, src + k, :], start=k == 0, stop=k == 3)
                elif SPLIT[b]:
                    in_ctx = args[-1] == "c"
                    n = N_CTX if in_ctx else SEQ
                    for k in range(KC):
                        if p == FIRST_U_PIECE[0] or p == FIRST_U_PIECE[1]:
                            pe.wait_ge(S["normed"], N_NORM_U[3 if b < B_GU2 else 8] - KC + k + 1)
                        hi, lo = (ctx_hi, ctx_lo) if in_ctx else (u_hi, u_lo)
                        last = mm3(bank(bk, 0, n), slot, k, hi[:, k, :], lo[:, k, :], k == 0, k == KC - 1)
                else:
                    if kind == "w_out" and args[0] == 0:
                        pe.wait_ge(S["branch_added"], 3 * KC)
                    if kind == "w_out2" and args[0] == 0:
                        pe.wait_ge(S["o_out"], 2 * HEADS + 4 + 2)
                        pe.wait_ge(S["gmlp_done"], 2)
                    x = {"mem_k": mem_n, "w_out": y_mix, "w_out2": yb}[kind]
                    n = N_MEM if kind == "mem_k" else SEQ
                    for k in range(KC):
                        last = mm(bank(bk, 0, n), tile_of(slot, k), x[:, k, :], start=k == 0, stop=k == KC - 1)
                last.then_inc(S[("split_used" if SPLIT[b] else "raw_used") if done else "half_mm"], 1)
                if kind == "w_out" and args[0]:
                    sum_chunk(4, args[0] - 1, 7, SEQ)

            def scores(t, sub):
                s = t.s0 + sub
                if t.kind == "c" and (sub or SOFT_TILE[s - 1].kind == "c"):
                    pe.wait_ge(S["exp_done"], s - 1)
                elif s > 0:
                    prev = SOFT_TILE[s - 1]
                    if prev.kind in ("dil", "a"):
                        pe.wait_ge(S["copied"], copied_before(s))
                    else:
                        pe.wait_ge(S["exp_done"], s)
                if t.kind == "mem":
                    if t.q == 0:
                        pe.wait_ge(S["piece_out"], 3 * t.head + 3)
                    last = mm(bank(2, 0, 256), mq[:, t.head, t.q * P:(t.q + 1) * P], mk[:, t.head, :],
                              start=True, stop=True)
                elif t.kind == "dil":
                    if t.q == 0:
                        pe.wait_ge(S["piece_out"], piece_count("dil_v", (t.head, 2)))
                        pe.wait_ge(S["hg_scored"], t.head + 1)
                        pe.wait_ge(S["hg_states"], t.head + 1)
                    rows = slice(t.q * P, (t.q + 1) * P)
                    mm(bank(2), dq[:, 0, rows], dk[:, 0, :], start=True, stop=True)
                    for g in (1, 2):
                        last = mm(bank(3, (g - 1) * P, P), dq[:, g, rows], dk[:, g, rows], start=True, stop=True)
                elif t.kind == "a":
                    j, par = t.head // 2, t.head % 2
                    part = slice(64 * par, 64 * par + 64)
                    if par == 0 and t.q == 0:
                        pe.wait_ge(S["roped"], 2 + j)
                        pe.wait_ge(S["piece_out"], piece_count("a_k", ("c",)))
                    lo, n = local_keys(t.q)
                    q = qa[part, j, t.q * P:(t.q + 1) * P]
                    mm(ps[:, 2, 0:n], q, ka[part, N_CTX + lo:N_CTX + lo + n], start=True, stop=True)
                    last = mm(ps[:, 3, 0:N_CTX], q, ka[part, 0:N_CTX], start=True, stop=True)
                else:
                    c, par = t.head // 2, t.head % 2
                    part = slice(64 * par + 32 * sub, 64 * par + 32 * sub + 32)
                    if par == 0 and t.q == 0 and sub == 0:
                        pe.wait_ge(S["roped"], 9)
                        pe.wait_ge(S["piece_out"], piece_count("b_u", (1,)))
                    q = qc[part, c, t.q * P:(t.q + 1) * P]
                    mm(ps[:, 2 - 2 * sub, :], q, kc[part, c, 0:SEQ], start=True, stop=True)
                    last = mm(ps[:, 3 - 2 * sub, 0:256], q, kc[part, c, SEQ:768], start=True, stop=True)
                last.then_inc(S["qk_mm"], 1)

            def turn(t):
                s = t.s0 + t.n_soft - 1
                if t.kind == "c":
                    pe.wait_ge(S["paired"], paired_before(t.index) + 1)
                else:
                    pe.wait_ge(S["scaled"], scaled_before(t.s0) + 1)
                if t.index:
                    pe.wait_ge(S["pt_act"], t.index)
                    if wide_before(t.index):
                        pe.wait_ge(S["pt_dve"], wide_before(t.index))
                if t.kind == "dil" and t.q == 0:
                    pe.wait_ge(S["hg_klt_done"], t.head + 1)
                    pe.wait_ge(S["hg_states"], t.head + 1)
                for k in range(t.n_keys):
                    last = nc.tensor.transpose(bank(4 + k // 4, (k % 4) * P, P), pr[:, s % 2, k * P:(k + 1) * P], ident)
                last.then_inc(S["transposed"], 1)

            def values(t):
                pe.wait_ge(S["pt_act"], t.index + 1)
                if t.n_keys > 4:
                    pe.wait_ge(S["pt_dve"], wide_before(t.index) + 1)
                first = t.index == 0 or TILES[t.index - 1].last
                if first and t.group:
                    pe.wait_ge(S["o_out"], t.group)
                if t.kind == "dil" and first:
                    pe.wait_ge(S["hg_done"], t.head + 1)
                if first and t.kind != "mem":
                    pe.wait_ge(S["turned"], {"dil": lambda: turn_count("dil_v", (t.head, 2)),
                                             "a": lambda: turn_count("a_v", ("c",)),
                                             "c": lambda: turn_count("c_v", (1, "c"))}[t.kind]())
                o_part = slice(0, P)
                for k in range(t.n_keys):
                    if t.kind == "mem":
                        v = mv[:, t.head, k, :]
                    elif t.kind == "dil":
                        v = dv[:, 0, k, :] if k < 4 else dv[:, k - 3, t.q, :]
                    elif t.kind == "a":
                        par = t.head % 2
                        o_part = slice(64 * par, 64 * par + 64)
                        lo, n = local_keys(t.q)
                        tok = 2 + lo // P + k if k < n // P else k - n // P
                        v = va[:, tok, 64 * par:64 * par + 64]
                    else:
                        par = t.head % 2
                        o_part = slice(64 * par, 64 * par + 64)
                        v = vc[:, k, t.head * 64:t.head * 64 + 64]
                    last = mm(ps[o_part, 6, t.q * P:(t.q + 1) * P], v, pt[:, t.index % 2, k * P:(k + 1) * P],
                              start=k == 0, stop=k == t.n_keys - 1)
                last.then_inc(S["pv_mm"], 1)

            def walk(steps):
                for st in steps:
                    name = st[0]
                    if name == "piece":
                        piece(st)
                    elif name == "attn":
                        pv, tr, qk = (TILES[i] if i is not None else None for i in st[1:])
                        if qk:
                            for sub in range(qk.n_soft):
                                scores(qk, sub)
                        if tr:
                            turn(tr)
                        if pv:
                            values(pv)
                    elif name == "turn":
                        _, i, p, kind, args = st
                        pe.wait_ge(S["piece_out"], p + 1)
                        pe.wait_ge(*bank7_free(st))
                        for t in range(2 if args[-1] == "c" else 4):
                            x = v_raw[:, i % 2, t:SEQ:4] if kind == "dil_v" else v_raw[:, i % 2, t * P:(t + 1) * P]
                            last = nc.tensor.transpose(bank(7, t * P, P), x, ident)
                        last.then_inc(S["turned_mm"], 1)
                    elif name == "hg_scores":
                        hd = st[1]
                        pe.wait_ge(S["hg_keys"], 2 * hd + 2)
                        pe.wait_ge(S["pt_act"], n_turned(st))
                        for t in range(4):
                            last = nc.tensor.transpose(bank(4, t * P, P), hg_kl[:, t * P:(t + 1) * P], ident)
                        last.then_inc(S["hg_turned"], 1)
                        pe.wait_ge(S["hg_queries"], 2 * hd + 2)
                        if hd:
                            pe.wait_ge(S["copied"], copied_before(n_scored(st)))
                        else:
                            pe.wait_ge(S["exp_done"], n_scored(st))
                        for t in range(4):
                            cs = slice(t * P, (t + 1) * P)
                            last = mm(bank(2, t * P, P), hg_ke[:, cs], hg_qe[:, cs], start=True, stop=True)
                        last.then_inc(S["hg_score_mm"], 1)
                    elif name == "hg_kv":
                        hd = st[1]
                        pe.wait_ge(S["hg_klt_done"], hd + 1)
                        pe.wait_ge(S["turned"], turn_count("hg_v", (hd,)))
                        if hd:
                            pe.wait_ge(S["pt_dve"], hd * 4)
                        for n in range(7):
                            part = slice(64 * (n % 2), 64 * (n % 2) + 64)
                            last = mm(bank(3 + 2 * (n % 2), (n // 2) * P, P), hg_klt[part, n // 2, :],
                                      hg_v[part, (n // 2) * P:(n // 2 + 1) * P], start=True, stop=True)
                        last.then_inc(S["hg_kv_mm"], 1)
                    elif name == "hg_out":
                        hd = st[1]
                        pe.wait_ge(S["hg_scored"], hd + 1)
                        pe.wait_ge(S["hg_states"], hd + 1)
                        pe.wait_ge(S["o_out"], n_groups(st))
                        for t in range(4):
                            cs = slice(t * P, (t + 1) * P)
                            mm(bank(6, t * P, P), hg_v[:, cs], hg_sc[:, cs], start=True, stop=False)
                            for n in (2 * t, 2 * t + 1):
                                if n:
                                    last = mm(bank(6, n * 64, 64), hg_state[:, n - 1, :], hg_qb[:, n * 64:(n + 1) * 64],
                                              start=False, stop=n == 2 * t + 1)
                        last.then_inc(S["hg_out_mm"], 1)
                    elif name == "hg_norm":
                        hd = st[1]
                        pe.wait_ge(S["hg_squares"], hd + 1)
                        pe.wait_ge(*bank7_free(st))
                        mm(bank(7), const("mean_128"), sq[:, 0, :], start=True, stop=True).then_inc(S["hg_mean"], 1)
                    elif name == "rope":
                        r = rope_index(st)
                        pe.wait_ge(S["act_link"], raw_count(st))
                        pe.wait_ge(*bank7_free(st))
                        w = const("swap16" if st[1] in ("ka", "qa") else "swap8")
                        mm(bank(7), w, raw[:, r % 2, 0:SEQ], start=True, stop=True).then_inc(S["swap_mm"], 1)
                    elif name == "diff_norm":
                        pe.wait_ge(S["diff_sq"], st[1] + 1)
                        pe.wait_ge(*bank7_free(st))
                        mm(bank(7), const("mean_64"), sq[:, 0, :], start=True, stop=True).then_inc(S["diff_mean"], 1)
                    elif name == "gmlp":
                        c = st[1]
                        pe.wait_ge(S["gelu_normed"], 1)
                        pe.wait_ge(*bank7_free(st))
                        for g in (2 * c, 2 * c + 1):
                            for t in range(4):
                                part = slice(64 * (g % 2), 64 * (g % 2) + 64)
                                last = mm(ps[part, 7, t * P:(t + 1) * P], vn[:, t, g * 64:g * 64 + 64], wst[:, g, :],
                                          start=True, stop=True)
                        last.then_inc(S["gmlp_mm"], 1)

            pe.wait_ge(S["tables1"], 32)
            walk(MIX1)
            sum_chunk(4, KC - 1, 7, SEQ)
            sums(5, 5, SEQ)

            for f in range(2):
                gate_up(1, f, f, B_GU2 + 4 * f, first=f == 0)
            with pe.Fori(0, 10) as i:
                for s in range(2):
                    b = B_GU2 + 8 + 4 * s
                    gate_up(1, 2 * i + 2 + s, s, b, i, 4)
            ffn_down(1, B_DN2)
            sums(6, 0, SEQ, [(S["y_moved"], 9)])
            sums(7, 7, N_CTX, [(S["y_moved"], 16)])
            sums(8, 5, SEQ)
            pe.wait_ge(S["tables2"], 80)
            walk(MIX2)

            sums(9, 7, SEQ)
            for k in range(KC):
                pe.wait_ge(S["normed"], N_NORM_U[9] - KC + k + 1)
                last = mm(ps[0:20, 6, :], router_w[:, k, :], u[:, k, :], start=k == 0, stop=k == KC - 1)
            last.then_inc(S["logits_mm"], 1)
            pe.wait_ge(S["logits_out"], 1)
            for t in range(4):
                last = nc.tensor.transpose(bank(7, 32 * t, 20), logits_t[:, t * P:(t + 1) * P], ident[0:20, 0:20])
            last.then_inc(S["route_mm"], 1)
            for t in range(4):
                for half in range(2):
                    i = 2 * t + half
                    if i >= 4:
                        pe.wait_ge(S["u_split"], i - 3)
                    for c in range(4):
                        last = nc.tensor.transpose(bank(i % 4, c * P, P), u[:, 4 * half + c, t * P:(t + 1) * P], ident)
                    last.then_inc(S["u_turned"], 1)
            pe.wait_ge(S["route_done"], 1)
            for t in range(4):
                for t2 in range(t):
                    mm(bank(5, 16 * t, 16), const("ones"), routed[:, t2, :], start=t2 == 0, stop=False)
                last = mm(bank(5, 16 * t, 16), const("before"), routed[:, t, :], start=t == 0, stop=True)
            last.then_inc(S["place_mm"], 1)
            for t in range(4):
                last = mm(bank(4, 0, 16), const("ones"), routed[:, t, :], start=t == 0, stop=t == 3)
            last.then_inc(S["count_mm"], 1)
            pe.wait_ge(S["count_mm"], 1)
            for name in ("he_turned", "back_mm", "sel_used"):
                pe.sem_inc(S[name], 1)
            pe.wait_ge(S["rounds_known"], 1)
            rounds = pe.alloc_register("rounds")
            pe.reg_load(rounds, rounds_i[0:1, 0:1])
            pe.wait_ge(S["u_split"], 8)

            with pe.Fori(0, rounds) as r:
                with pe.Fori(0, N_EXP // GROUP) as g:
                    G = 4 * r + g
                    pe.wait_ge(S["sel_done"], G + 1)
                    for c in range(KC):
                        if c < 2:
                            pe.wait_ge(S["back_added"], 32 * G + 1)
                        else:
                            pe.wait_ge(S["xe_out"], 8 * G + c - 1)
                        for t in range(4):
                            x = slice(c * P, (c + 1) * P)
                            mm(bank(5 + c % 2), t_hi[:, t, x], sel[:, :, t, :], start=t == 0, stop=False)
                            last = mm(bank(5 + c % 2), t_lo[:, t, x], sel[:, :, t, :], start=False, stop=t == 3)
                        last.then_inc(S["xe_mm"], 1)
                        if c % 2 == 1:
                            q = c // 2
                            pe.wait_ge(S["selt_out"], 4 * G + q + 1)
                            for t in range(4):
                                last = nc.tensor.transpose(bank(7, t * P, P), sel[:, q, t, :].bitcast(F32), ident)
                            last.then_inc(S["selt_mm"], 1)
                    pe.wait_ge(S["he_moved"], 4 * G + 1)
                    for q in range(GROUP):
                        for t in range(4):
                            last = mm(bank(2, q, 1), sel[:, q, t, :].bitcast(F32), gates_e[:, bass.ds(4 * g + q, 1), t],
                                      start=t == 0, stop=t == 3)
                    last.then_inc(S["gsel_mm"], 1)
                    pe.wait_ge(S["gsel_mm"], G + 1)
                    pe.sem_inc(S["sel_used"], 1)
                    pe.wait_ge(S["xe_out"], 8 * G + 8)

                    def add_back(q, c):
                        if c == 0:
                            pe.wait_ge(S["y_lo_done"], 8 * G + 2 * q + 4)
                            pe.wait_ge(S["selt_out"], 4 * G + q + 2)
                        if q or c >= 2:
                            pe.wait_ge(S["back_added"], 32 * G + 8 * q + c)
                        x = slice(c * P, (c + 1) * P)
                        mm(bank(5 + c % 2), y_hi[:, x], sel_t[:, q, :], start=True, stop=False)
                        last = mm(bank(5 + c % 2), y_lo[:, x], sel_t[:, q, :], start=False, stop=True)
                        last.then_inc(S["back_mm"], 1)

                    for q in range(GROUP):
                        pe.wait_ge(S["he_done"], 4 * G + q + 1)
                        for j in range(8):
                            pe.wait_ge(landed[j % SLOTS], 16 * ((B_MOE + 12 * q + j) // SLOTS + 1) + 768 * r + 192 * g)
                            for k in range(2):
                                kt = 2 * (j // 2) + k
                                last = mm(bank(j % 2), xe[:, kt, q * P:(q + 1) * P],
                                          ring[:, j % SLOTS, k * SEQ:(k + 1) * SEQ], start=kt == 0, stop=kt == KC - 1)
                            last.then_inc(S["raw_used"], 1)
                            if q and 2 <= j < 2 + EARLY:
                                add_back(q - 1, j - 2)
                        if q:
                            add_back(q - 1, EARLY)
                        pe.wait_ge(S["he_done"], 4 * G + q + 2)
                        if q == 0:
                            pe.wait_ge(S["gsel_out"], G + 1)
                        pe.wait_ge(S["he_moved"], 4 * G + q + 1)
                        for k in range(4):
                            last = nc.tensor.transpose(bank(2, k * P, P), he[:, k * P:(k + 1) * P], ident)
                        last.then_inc(S["he_turned"], 1)
                        if q:
                            for c in range(EARLY + 1, KC):
                                add_back(q - 1, c)
                        pe.wait_ge(S["he_moved"], 4 * G + q + 2)
                        pe.wait_ge(S["y_lo_done"], 8 * G + 2 * q + 2)
                        for k in range(4):
                            pe.wait_ge(landed[k], 16 * ((B_MOE + 12 * q + 8) // SLOTS + 1) + 768 * r + 192 * g)
                            for half in range(2):
                                last = mm(bank(3 + half), he_t[:, k, :], ring[:, k, half * SEQ:(half + 1) * SEQ],
                                          start=k == 0, stop=k == 3)
                            last.then_inc(S["raw_used"], 1)
                    for c in range(KC):
                        add_back(GROUP - 1, c)
                pe.reg_load(rounds, rounds_i[0:1, 0:1])
            sums(10, 0, SEQ)

        @block.scalar
        def _(act):
            fn = nc.scalar.activation

            def squares(m, src, n, ready):
                for k in range(KC):
                    ready(k)
                    if KC * m + k >= 2:
                        act.wait_ge(S["sum_done"], KC * m + k - 1)
                    fn(sq[:, k % 2, 0:n], src(k), ACT.Square).then_inc(S["sq_done"], 1)

            def root(m, bk, n):
                act.wait_ge(S["sum_done"], KC * m + KC)
                if m:
                    act.wait_ge(S["inv_done"], m)
                fn(rms[:, 0:n], bank(bk, 0, n), ACT.Sqrt, bias=eps_col).then_inc(S["root_done"], 1)

            def high_parts(j):
                for k in range(KC):
                    act.wait_ge(S["chunk_made"], KC * j + k + 1)
                    fn(u_hi[:, k, :], hidden_t[:, k % 2, :], ACT.Copy).then_inc(S["high_made"], 1)

            act.wait_ge(S["params"], 80)
            act.wait_ge(S["prep_dve"], 2)
            fn(lbt[:, 4:12], lbt[:, 4:12], ACT.Exp).then_inc(S["prep_act"], 1)
            act.wait_ge(S["prep_pe"], 1)
            fn(lam_e, bank(6, 0, 2), ACT.Exp).then_inc(S["prep_act"], 1)
            squares(0, lambda k: mem_raw[:, k, :], N_MEM, lambda k: None)
            root(0, 7, N_MEM)
            squares(1, lambda k: h[:, k, :], SEQ, lambda k: None)
            root(1, 5, SEQ)
            high_parts(0)

            def silu_gate(j, f, q):
                fi = NF * j + f
                act.wait_ge(S["split_used"], index_of((B_GU1, B_GU2 + 1)[j]) + 2 * f + 1)
                act.wait_ge(S["act_done"], fi + 1)
                fn(silu_g[:, q, :], bank(2 * q), ACT.Silu).then_inc(S["silu_done"], 1)

            with act.Fori(0, NF // 2) as i:
                for q in range(2):
                    silu_gate(0, 2 * i + q, q)

            def ffn_post(j, m):
                squares(m, ysb, SEQ, lambda k: act.wait_ge(S["y_moved"], KC * j + k + 1))
                root(m, 0, SEQ)

            ffn_post(0, 2)
            squares(3, lambda k: h[:, k, :], SEQ, lambda k: act.wait_ge(S["h_done"], k + 1))
            root(3, 7, SEQ)
            high_parts(1)

            def piece(st):
                _, p, b, kind, args, done = st
                if kind == "branch" or kind == "w_out2":
                    return
                act.wait_ge(*piece_done(st))
                if p:
                    act.wait_ge(S["piece_out"], p)
                src, func, bias = bank(p % 2), ACT.Copy, 0.0
                if kind == "mem_k":
                    dst, src = mk[:, args[0], :], bank(p % 2, 0, N_MEM)
                elif kind == "mem_v":
                    dst, src = mv[:, args[0], :, :].rearrange("p a b -> p (a b)"), bank(p % 2, 0, 256)
                elif kind == "mem_q":
                    dst = mq[:, args[0], :]
                elif kind in VALUE_KINDS:
                    i = turn_count(kind, args) - 1
                    if i >= 2:
                        act.wait_ge(S["turned_mm"], i - 1)
                    n = N_CTX if args[-1] == "c" else SEQ
                    dst, src = v_raw[:, i % 2, 0:n], bank(p % 2, 0, n)
                elif kind in ("hg_f", "hg_q", "hg_og"):
                    if args[0]:
                        act.wait_ge(S["hg_done"], args[0])
                    dst = {"hg_f": hg_sg, "hg_q": hg_q, "hg_og": hg_og}[kind]
                    func = {"hg_f": ACT.Sigmoid, "hg_q": ACT.Silu, "hg_og": ACT.Sigmoid}[kind]
                elif kind in ("dil_q", "dil_k"):
                    hd, g = args
                    if hd:
                        act.wait_ge(S["qk_mm"], 16 + 4 * hd)
                    dst = {"dil_q": dq, "dil_k": dk}[kind][:, g, :].rearrange("p (r l) -> p r l", r=4)
                    src = src.rearrange("p (l r) -> p r l", r=4)
                elif kind == "gate":
                    b_at = {"hg": 0, "dil": 8, "mem": 16}[args[0]] + args[1]
                    if branch_index(args) >= 2:
                        act.wait_ge(S["branch_added"], branch_index(args) - 1)
                    dst, func, bias = tmp[:, args[1] % 2, :], ACT.Sigmoid, col("b_gate", b_at)
                elif kind == "w_out":
                    n = args[0]
                    act.wait_ge(S["sum_done"], KC * 4 + n - 1)
                    fn(sq[:, n % 2, :], src, ACT.Square).then_inc(S["sq_done"], 1)
                    dst = w_out_y[:, n, :]
                elif kind == "a_k" or kind == "c_k":
                    is_a = kind == "a_k"
                    if args[-1] == "x":
                        r = rope_index(("rope", "ka", 0) if is_a else ("rope", "kc", args[0]))
                        if r >= 2:
                            act.wait_ge(S["roped"], r - 1)
                        fn(raw[:, r % 2, 0:SEQ], src, ACT.Copy).then_inc(S["act_link"], 1)
                        act.wait_ge(S["act_link"], raw_count(("rope", "ka" if is_a else "kc", 0 if is_a else args[0])))
                        act.sem_inc(S["piece_out"], 1)
                        return
                    dst = ka[:, 0:N_CTX] if is_a else kc[:, args[0], 0:N_CTX]
                    src = bank(p % 2, 0, N_CTX)
                elif kind in ("a_q", "c_q"):
                    st_r = ("rope", "qa" if kind == "a_q" else "qc", args[0])
                    r = rope_index(st_r)
                    if r >= 2:
                        act.wait_ge(S["roped"], r - 1)
                    fn(raw[:, r % 2, 0:SEQ], src, ACT.Copy).then_inc(S["act_link"], 1)
                    act.wait_ge(S["act_link"], raw_count(st_r))
                    act.sem_inc(S["piece_out"], 1)
                    return
                elif kind == "b_u":
                    dst, func = ub[:, args[0], :], ACT.Gelu_apprx_tanh
                fn(dst, src, func, bias=bias).then_inc(S["piece_out"], 1)

            def turned(st):
                _, i, p, kind, args = st
                act.wait_ge(S["turned_mm"], i + 1)
                src, func = bank(7), ACT.Copy
                if kind == "hg_v":
                    if args[0]:
                        act.wait_ge(S["hg_done"], args[0])
                    dst = hg_v
                elif kind == "dil_v":
                    if args[0]:
                        act.wait_ge(S["pv_mm"], 16 + 4 * args[0])
                    dst = dv[:, args[1], :, :].rearrange("p a b -> p (a b)")
                elif kind == "a_v":
                    if args[0] == "x":
                        dst = va[:, 2:6, :].rearrange("p a b -> p (a b)")
                    else:
                        dst, src = va[:, 0:2, :].rearrange("p a b -> p (a b)"), bank(7, 0, N_CTX)
                elif kind == "c_v":
                    part = slice(args[0] * P, (args[0] + 1) * P)
                    if args[1] == "x":
                        dst, src = vc[:, 2:6, part], src.rearrange("p (a b) -> p a b", b=P)
                    else:
                        dst, src = vc[:, 0:2, part], bank(7, 0, N_CTX).rearrange("p (a b) -> p a b", b=P)
                else:
                    dst, func = vf[:, :, args[0] * P:(args[0] + 1) * P], ACT.Gelu_apprx_tanh
                    src = src.rearrange("p (a b) -> p a b", b=P)
                fn(dst, src, func).then_inc(S["turned"], 1)

            def soft(t, sub):
                s = t.s0 + sub
                act.wait_ge(S["shift_done"], s + 1)
                if s >= 2:
                    prev = SOFT_TILE[s - 2]
                    if prev.kind == "c" and s % 2 == 0:
                        act.wait_ge(S["paired"], paired_before(prev.index) + 1)
                    else:
                        act.wait_ge(S["transposed"], prev.index + 1)
                    act.wait_ge(S["rden_done"], s - 1)
                w = t.width
                if t.kind in ("dil", "a"):
                    src = sc[:, 0:w]
                else:
                    src = ps[:, 2 - 2 * sub:4 - 2 * sub, :].rearrange("p a b -> p (a b)")[:, 0:w]
                scale = {"mem": P, "dil": P, "a": 64, "c": 32}[t.kind] ** -0.5
                if t.kind == "a":
                    hd = a_head(t)
                    fn(es[:, s % 2:s % 2 + 1], col("sink", hd), ACT.Exp,
                       bias=negm[:, s % 2:s % 2 + 1]).then_inc(S["act_link"], 1)
                    act.wait_ge(S["act_link"], N_ROPE_RAW_BEFORE_A[t.index])
                fn(pr[:, s % 2, 0:w], src, ACT.Exp, bias=negm[:, s % 2:s % 2 + 1], scale=scale,
                   accum_out=den[:, s % 2:s % 2 + 1]).then_inc(S["exp_done"], 1)

            def move_pt(t):
                act.wait_ge(S["transposed"], t.index + 1)
                if t.index >= 2:
                    act.wait_ge(S["pv_mm"], t.index - 1)
                n = min(t.n_keys, 4) * P
                fn(pt[:, t.index % 2, 0:n], bank(4, 0, n), ACT.Copy).then_inc(S["pt_act"], 1)

            def move_out(t):
                act.wait_ge(S["pv_mm"], t.index + 1)
                if t.kind == "mem":
                    fn(yb[:, 8 + t.head, :], bank(6), ACT.Copy).then_inc(S["o_out"], 1)
                elif t.kind == "dil":
                    fn(yb[:, 4 + t.head, :].rearrange("p (l r) -> p r l", r=4),
                       bank(6).rearrange("p (r l) -> p r l", r=4), ACT.Copy).then_inc(S["o_out"], 1)
                elif t.kind == "a":
                    fn(yb[:, t.head // 2, :], bank(6), ACT.Copy).then_inc(S["o_out"], 1)

            def walk(steps):
                for st in steps:
                    name = st[0]
                    if name == "piece":
                        piece(st)
                    elif name == "attn":
                        pv, tr, qk = (TILES[i] if i is not None else None for i in st[1:])
                        if qk:
                            soft(qk, 0)
                        if tr:
                            move_pt(tr)
                        if qk and qk.n_soft == 2:
                            soft(qk, 1)
                        if pv and pv.last and pv.kind != "c":
                            move_out(pv)
                    elif name == "turn":
                        turned(st)
                    elif name == "hg_front":
                        hd = st[1]
                        act.wait_ge(S["hg_f_done"], hd + 1)
                        fn(hg_b, hg_sg, ACT.Ln).then_inc(S["hg_ln_done"], 1)
                        act.wait_ge(S["hg_shifted"], hd + 1)
                        fn(hg_qe, hg_t, ACT.Exp).then_inc(S["hg_exps"], 1)
                        fn(hg_ke, hg_t, ACT.Exp, scale=-1.0).then_inc(S["hg_exps"], 1)
                        fn(hg_kl, hg_t2, ACT.Exp, scale=-1.0).then_inc(S["hg_exps"], 1)
                        fn(hg_qb, hg_sg, ACT.Exp).then_inc(S["hg_exps"], 1)
                        fn(hg_dec, hg_sg.rearrange("p (n c) -> p n c", c=64)[:, :, 63], ACT.Exp
                           ).then_inc(S["hg_exps"], 1)
                    elif name == "hg_scores":
                        act.wait_ge(S["hg_turned"], st[1] + 1)
                        fn(hg_klt.rearrange("p a b -> p (a b)"), bank(4), ACT.Copy).then_inc(S["hg_klt_done"], 1)
                    elif name == "hg_norm":
                        hd = st[1]
                        act.wait_ge(S["hg_out_mm"], hd + 1)
                        fn(sq[:, 0, :], bank(6), ACT.Square).then_inc(S["hg_squares"], 1)
                        act.wait_ge(S["hg_mean"], hd + 1)
                        if hd:
                            act.wait_ge(S["hg_done"], hd)
                        fn(rms[:], bank(7), ACT.Sqrt, bias=eps_col).then_inc(S["hg_root"], 1)
                    elif name == "diff_norm":
                        c = st[1]
                        act.wait_ge(S["pv_mm"], last_c_tile(c) + 1)
                        fn(sq[:, 0, :], bank(6), ACT.Square).then_inc(S["diff_sq"], 1)
                        act.wait_ge(S["diff_mean"], c + 1)
                        fn(rms[:], bank(7), ACT.Sqrt, bias=eps_col).then_inc(S["diff_root"], 1)
                    elif name == "gmlp_norm":
                        act.wait_ge(S["gelu_norm_in"], 1)
                        fn(gm_var, gm_var, ACT.Sqrt, bias=eps_col, scale=1.0 / 64).then_inc(S["gelu_root"], 1)

            walk(MIX1)
            root(4, 7, SEQ)
            squares(5, lambda k: h[:, k, :], SEQ, lambda k: act.wait_ge(S["h_done"], N_H[2] + k + 1))
            root(5, 5, SEQ)
            high_parts(2)
            act.wait_ge(S["c_in"], 16)
            fn(c_rows, c_rows, ACT.Silu).then_inc(S["c_silu"], 1)
            act.sem_inc(S["x_summed"], 1)
            act.sem_inc(S["ctx_summed"], 1)

            def ada_sums(n, with_ctx):
                if with_ctx:
                    act.wait_ge(S["ada_ctx"], n + 1)
                    fn(ada_prod[:, 1, :], ada_prod[:, 1, :], ACT.Copy, accum_out=mod[:, bass.ds(2 * n + 1, 1)]
                       ).then_inc(S["ctx_summed"], 1)
                act.wait_ge(S["ada_x"], n + 1)
                fn(ada_prod[:, 0, :], ada_prod[:, 0, :], ACT.Copy, accum_out=mod[:, bass.ds(2 * n, 1)]
                   ).then_inc(S["x_summed"], 1)

            for lo, hi in ((0, N_ADA_CTX // 4), (N_ADA_CTX // 4, NF // 2)):
                with act.Fori(lo, hi) as i:
                    for q in range(2):
                        for w in range(2):
                            ada_sums(4 * i + 2 * q + w, lo == 0)
                        silu_gate(1, 2 * i + q, q)
            for n in range(2 * NF, 48):
                ada_sums(n, False)
            ffn_post(1, 6)
            act.wait_ge(S["ctx_in"], 16)
            squares(7, lambda k: ctx_raw[:, k, :], N_CTX, lambda k: None)
            root(7, 7, N_CTX)
            squares(8, lambda k: h[:, k, :], SEQ, lambda k: act.wait_ge(S["h_done"], N_H[6] - 8 + k + 1))
            root(8, 5, SEQ)
            high_parts(3)
            walk(MIX2)
            squares(9, lambda k: h[:, k, :], SEQ, lambda k: act.wait_ge(S["x_res"], k + 1))
            root(9, 7, SEQ)
            def high_half(i):
                act.wait_ge(S["u_turned"], i + 1)
                fn(t_hi[:, i // 2, (i % 2) * SEQ:(i % 2 + 1) * SEQ], bank(i % 4), ACT.Copy).then_inc(S["u_hi_done"], 1)

            act.wait_ge(S["logits_mm"], 1)
            fn(logits_t, ps[0:20, 6, :], ACT.Copy).then_inc(S["logits_out"], 1)
            for i in range(4):
                high_half(i)
            act.wait_ge(S["route_exp_in"], 1)
            fn(rt[:, 80:96], rt[:, 80:96], ACT.Exp).then_inc(S["route_exp"], 1)
            act.wait_ge(S["route_e2_in"], 1)
            fn(rt[:, 200:204], rt[:, 200:204], ACT.Exp).then_inc(S["route_exp"], 1)
            for i in range(4, 8):
                high_half(i)
            act.sem_inc(S["selt_out"], 1)
            act.sem_inc(S["he_moved"], 1)
            act.wait_ge(S["rounds_known"], 1)
            rounds = act.alloc_register("rounds")
            act.reg_load(rounds, rounds_i[0:1, 0:1])
            with act.Fori(0, rounds) as r:
                with act.Fori(0, N_EXP // GROUP) as g:
                    G = 4 * r + g
                    act.wait_ge(S["he_done"], 4 * G + 1)
                    for c in range(KC):
                        act.wait_ge(S["xe_mm"], 8 * G + c + 1)
                        fn(xe[:, c, :], bank(5 + c % 2), ACT.Copy).then_inc(S["xe_out"], 1)
                        if c % 2 == 1:
                            q = c // 2
                            if q == 0:
                                act.wait_ge(S["back_mm"], 32 * G + 1)
                            act.wait_ge(S["selt_mm"], 4 * G + q + 1)
                            fn(sel_t[:, q, :], bank(7), ACT.Copy).then_inc(S["selt_out"], 1)
                    for q in range(GROUP):
                        R = index_of(B_MOE) + 12 * q
                        act.wait_ge(S["raw_used"], R + 7 + 192 * r + 48 * g)
                        act.wait_ge(S["he_done"], 4 * G + q + 1)
                        fn(moe_silu, bank(0), ACT.Silu).then_inc(S["silu_e"], 1)
                        act.wait_ge(S["he_turned"], 4 * G + q + 2)
                        fn(he_t.rearrange("p a b -> p (a b)"), bank(2), ACT.Copy).then_inc(S["he_moved"], 1)
                        act.wait_ge(S["raw_used"], R + 12 + 192 * r + 48 * g)
                        act.wait_ge(S["back_mm"], 32 * G + 8 * q + 1)
                        for half in range(2):
                            fn(y_hi[:, half * SEQ:(half + 1) * SEQ], bank(3 + half), ACT.Copy
                               ).then_inc(S["y_hi_done"], 1)
            squares(10, lambda k: h[:, k, :], SEQ, lambda k: act.wait_ge(S["x_res"], KC + k + 1))
            root(10, 0, SEQ)

        @block.gpsimd
        def _(pool):
            tt, ts = nc.gpsimd.tensor_tensor, nc.gpsimd.tensor_scalar
            nc.gpsimd.memset(zero[:], 0.0).then_inc(S["absorbed"], 1)
            pool.wait_ge(S["absorbed"], 1)

            def split(b, turns=0, step=0):
                n = index_of(b)
                slot, part = b % SLOTS, n % SPLIT_SLOTS
                pool.wait_ge(landed[slot], 16 * (b // SLOTS + 1) + 16 * turns)
                if n >= SPLIT_SLOTS:
                    pool.wait_ge(S["split_used"], n + 1 - SPLIT_SLOTS + step * turns)
                tt(zero[:, 1:2], zero[:, 0:1], zero[:, 0:1], ALU.mult).then_inc(S["absorbed"], 1)
                ts(w_hi[:, part, :], ring[:, slot, :], 1.0, 1.0, ALU.mult, ALU.mult).then_inc(S["split_hi"], 1)
                pool.wait_ge(S["split_hi"], n + 1 + step * turns)
                tt(w_lo[:, part, :], ring[:, slot, :], w_hi[:, part, :].bitcast(F32), ALU.subtract
                   ).then_inc(S["split_done"], 1)

            def split_all(lo, hi):
                n = (hi - lo) // SLOTS
                with pool.Fori(0, n) as i:
                    for b in range(lo, lo + SLOTS):
                        split(b, turns=i, step=SLOTS)
                for b in range(lo + SLOTS * n, hi):
                    split(b)

            for b in range(SPLIT_SLOTS):
                split(b)
            split_all(SPLIT_SLOTS, B_MIX1)
            for b in range(B_MIX1, B_GU2):
                if SPLIT[b]:
                    split(b)
            with pool.Fori(0, NF) as i:
                for b in (B_GU2 + 1, B_GU2 + 3):
                    split(b, turns=i, step=2)
            split_all(B_DN2, B_MIX2)
            for b in range(B_MIX2, B_MOE):
                if SPLIT[b]:
                    split(b)

        @block.vector
        def _(dve):
            v = nc.vector
            links = [0]

            def link(ins):
                links[0] += 1
                ins.then_inc(S["dve_link"], 1)
                dve.wait_ge(S["dve_link"], links[0])

            def invert(m, n):
                dve.wait_ge(S["root_done"], m + 1)
                v.reciprocal(rinv[:, 0:n], rms[:, 0:n]).then_inc(S["inv_done"], 1)
                dve.wait_ge(S["inv_done"], m + 1)

            def normalise_split(j, src, w, shift=None):
                def low(k):
                    dve.wait_ge(S["high_made"], KC * j + k + 1)
                    v.tensor_tensor(u_lo[:, k, :], hidden_t[:, k % 2, :], u_hi[:, k, :].bitcast(F32), ALU.subtract
                                    ).then_inc(S["normed"], 1)

                for k in range(KC):
                    x = hidden_t[:, k % 2, :]
                    if k >= 2:
                        dve.wait_ge(S["normed"], N_NORM_U[(1, 3, 5, 8)[j]] - KC + k - 1)
                    ins = v.scalar_tensor_tensor(out=x, in0=src(k), scalar=w(k), in1=rinv[:], op0=ALU.mult, op1=ALU.mult)
                    if shift is not None:
                        link(ins)
                        ins = v.tensor_scalar(x, x, shift(k), None, ALU.add)
                    ins.then_inc(S["chunk_made"], 1)
                    if k:
                        low(k - 1)
                low(KC - 1)

            def normalise_context(dst_hi, dst_lo, src, w, n, shift=None):
                for k in range(KC):
                    x = hidden_t[:, k % 2, 0:n]
                    link(v.scalar_tensor_tensor(out=x, in0=src(k), scalar=w(k), in1=rinv[:, 0:n], op0=ALU.mult,
                                                op1=ALU.mult))
                    if shift is not None:
                        link(v.tensor_scalar(x, x, shift(k), None, ALU.add))
                    link(v.tensor_scalar(dst_hi[:, k, :], x, 1.0, None, ALU.mult))
                    v.tensor_tensor(dst_lo[:, k, :], x, dst_hi[:, k, :].bitcast(F32), ALU.subtract
                                    ).then_inc(S["normed"], 1)

            def normalise(dst, src, w, n, shift=None):
                for k in range(KC):
                    ins = v.scalar_tensor_tensor(out=dst(k), in0=src(k), scalar=w(k), in1=rinv[:, 0:n], op0=ALU.mult,
                                                 op1=ALU.mult)
                    if shift is None:
                        ins.then_inc(S["normed"], 1)
                    else:
                        link(ins)
                        v.tensor_scalar(dst(k), dst(k), shift(k), None, ALU.add).then_inc(S["normed"], 1)

            def add_normed(name, src, half, count):
                for k in range(KC):
                    link(v.scalar_tensor_tensor(out=tmp[:, k % 2, :], in0=src(k), scalar=col(name, k), in1=rinv[:],
                                                op0=ALU.mult, op1=ALU.mult))
                    v.scalar_tensor_tensor(out=h[:, k, :], in0=tmp[:, k % 2, :], scalar=half, in1=h[:, k, :],
                                           op0=ALU.mult, op1=ALU.add).then_inc(S["h_done"], 1)

            v.memset(eps_col, EPS).then_inc(S["act_done"], 1)
            v.memset(hg_dec, 0.0).then_inc(S["act_done"], 1)
            dve.wait_ge(S["act_done"], 2)
            dve.wait_ge(S["params"], 80)
            lam = col("lam", 0, 4)
            v.tensor_tensor(lam_p[0:32, :], lam[0:32, 0:2], lam[0:32, 2:4], ALU.mult).then_inc(S["prep_dve"], 1)
            l0, l1 = col("hg_lb0", 0, 4), col("hg_lb1", 0, 4)
            link(v.tensor_tensor(lbt[:, 0:4], l0, l1, ALU.max))
            link(v.tensor_tensor(lbt[:, 4:8], l0, lbt[:, 0:4], ALU.subtract))
            v.tensor_tensor(lbt[:, 8:12], l1, lbt[:, 0:4], ALU.subtract).then_inc(S["prep_dve"], 1)
            dve.wait_ge(S["prep_act"], 1)
            link(v.tensor_tensor(lbt[:, 0:4], lbt[:, 4:8], lbt[:, 8:12], ALU.add))
            link(v.reciprocal(lbt[:, 0:4], lbt[:, 0:4]))
            link(v.tensor_tensor(lb, lbt[:, 4:8], lbt[:, 0:4], ALU.mult))
            link(v.tensor_scalar(omlb, lb, -1.0, 1.0, ALU.mult, ALU.add))
            dve.wait_ge(S["prep_act"], 2)
            link(v.tensor_tensor(lam_neg, lam_e[:, 1:2], lam_e[:, 0:1], ALU.subtract))
            link(v.tensor_scalar(lam_neg, lam_neg, -LAM_INIT, None, ALU.add))
            invert(0, N_MEM)
            normalise(lambda k: mem_n[:, k, :], lambda k: mem_raw[:, k, :], lambda k: col("mem_norm", k), N_MEM)
            dve.wait_ge(S["normed"], 8)
            invert(1, SEQ)
            normalise_split(0, lambda k: h[:, k, :], lambda k: col("ffn1_pre", k))
            dve.wait_ge(S["normed"], 16)

            def hidden(j, f, q):
                fi = NF * j + f
                dve.wait_ge(S["split_used"], index_of((B_GU1, B_GU2 + 1)[j]) + 2 * f + 2)
                dve.wait_ge(S["silu_done"], fi + 1)
                v.tensor_tensor(hidden_t[:, q, :], silu_g[:, q, :], bank(2 * q + 1), ALU.mult
                                ).then_inc(S["hidden_made"], 1)
                dve.wait_ge(S["hidden_made"], fi + 1)
                v.tensor_scalar(act_hi[:, bass.ds(f * SEQ, SEQ)], hidden_t[:, q, :], 1.0, None, ALU.mult
                                ).then_inc(S["hi_made"], 1)
                dve.wait_ge(S["hi_made"], fi + 1)
                v.tensor_tensor(act_lo[:, bass.ds(f * SEQ, SEQ)], hidden_t[:, q, :],
                                act_hi[:, bass.ds(f * SEQ, SEQ)].bitcast(F32), ALU.subtract).then_inc(S["act_done"], 1)

            def ffn_out(j, m, name):
                for n in range(KC):
                    dve.wait_ge(S["down_mm"], KC * j + n + 1)
                    v.tensor_copy(ysb(n), bank(n)).then_inc(S["y_moved"], 1)
                dve.wait_ge(S["y_moved"], KC * (j + 1))
                invert(m, SEQ)
                add_normed(name, ysb, 0.5, m)

            with dve.Fori(0, NF // 2) as i:
                for q in range(2):
                    hidden(0, 2 * i + q, q)
            ffn_out(0, 2, "ffn1_post")
            dve.wait_ge(S["h_done"], N_H[2])
            invert(3, SEQ)
            normalise_split(1, lambda k: h[:, k, :], lambda k: col("mix_pre", k))
            dve.wait_ge(S["tables1"], 32)
            v.memset(hg_sc, 0.0).then_inc(S["prep_dve"], 1)
            dve.wait_ge(S["prep_dve"], 3)

            def shift(t, sub):
                s = t.s0 + sub
                b = slice(s % 2, s % 2 + 1)
                w = t.width
                scale = {"mem": P, "dil": P, "a": 64, "c": 32}[t.kind] ** -0.5
                dve.wait_ge(S["qk_mm"], s + 1)
                if t.kind == "c" and s >= 2:
                    dve.wait_ge(S["exp_done"], s - 1)
                elif s >= 1:
                    dve.wait_ge(S["exp_done"], s)
                if t.kind == "dil":
                    for g, lo, n, src in ((0, 0, SEQ, bank(2)), (1, SEQ, P, bank(3, 0, P)), (2, SEQ + P, P, bank(3, P, P))):
                        ins = v.scalar_tensor_tensor(out=sc[:, lo:lo + n], in0=dist[:, t.q, lo:lo + n],
                                                     scalar=-slope(g, t.head) / scale, in1=src, op0=ALU.mult,
                                                     op1=ALU.add)
                    link(ins)
                    src = sc[:, 0:w]
                elif t.kind == "a":
                    lo, n = local_keys(t.q)
                    off = lo - (t.q - 1) * P
                    v.scalar_tensor_tensor(out=sc[:, 0:n], in0=const("window", off, n), scalar=1.0,
                                           in1=ps[:, 2, 0:n], op0=ALU.mult, op1=ALU.add)
                    link(v.tensor_copy(sc[:, n:n + N_CTX], ps[:, 3, 0:N_CTX]))
                    src = sc[:, 0:w]
                else:
                    src = ps[:, 2 - 2 * sub:4 - 2 * sub, :].rearrange("p a b -> p (a b)")[:, 0:w]
                if t.kind in ("dil", "a"):
                    dve.sem_inc(S["copied"], 1)
                if s >= 2:
                    dve.wait_ge(S["rden_done"], s - 1)
                link(v.tensor_reduce(mx[:, b], src, AX, ALU.max))
                if t.kind == "a":
                    hd = a_head(t)
                    link(v.tensor_scalar(mx[:, b], mx[:, b], scale, col("sink", hd), ALU.mult, ALU.max))
                    v.tensor_scalar(negm[:, b], mx[:, b], -1.0, None, ALU.mult).then_inc(S["shift_done"], 1)
                else:
                    v.tensor_scalar(negm[:, b], mx[:, b], -scale, None, ALU.mult).then_inc(S["shift_done"], 1)

            def weigh(t, sub):
                s = t.s0 + sub
                b = slice(s % 2, s % 2 + 1)
                w = t.width
                dve.wait_ge(S["exp_done"], s + 1)
                if t.kind == "a":
                    link(v.tensor_tensor(den[:, b], den[:, b], es[:, b], ALU.add))
                v.reciprocal(rden[:, b], den[:, b]).then_inc(S["rden_done"], 1)
                dve.wait_ge(S["rden_done"], s + 1)
                if not (t.kind == "c" and sub == 1):
                    v.tensor_scalar(pr[:, s % 2, 0:w], pr[:, s % 2, 0:w], rden[:, b], None, ALU.mult
                                    ).then_inc(S["scaled"], 1)
                else:
                    link(v.tensor_tensor(rden[:, b], rden[:, b], lam_neg, ALU.mult))
                    dve.wait_ge(S["scaled"], scaled_before(s))
                    v.scalar_tensor_tensor(out=pr[:, 1, 0:w], in0=pr[:, 1, 0:w], scalar=rden[:, b], in1=pr[:, 0, 0:w],
                                           op0=ALU.mult, op1=ALU.add).then_inc(S["paired"], 1)

            def move_pt(t):
                if t.n_keys <= 4:
                    return
                dve.wait_ge(S["transposed"], t.index + 1)
                if t.index >= 2:
                    dve.wait_ge(S["pv_mm"], t.index - 1)
                n = (t.n_keys - 4) * P
                v.tensor_copy(pt[:, t.index % 2, SEQ:SEQ + n], bank(5, 0, n)).then_inc(S["pt_dve"], 1)

            def piece(st):
                _, p, b, kind, args, done = st
                if kind == "branch":
                    i = branch_index(args)
                    dve.wait_ge(*piece_done(st))
                    dve.wait_ge(S["piece_out"], p)
                    if args[0] == "mem":
                        ins = v.tensor_tensor(y_mix[:, args[1], :], bank(p % 2), tmp[:, args[1] % 2, :], ALU.mult)
                    else:
                        dve.wait_ge(S["branch_added"], i)
                        link(v.tensor_tensor(tmp[:, args[1] % 2, :], bank(p % 2), tmp[:, args[1] % 2, :], ALU.mult))
                        ins = v.tensor_tensor(y_mix[:, args[1], :], tmp[:, args[1] % 2, :], y_mix[:, args[1], :], ALU.add)
                    ins.then_inc(S["branch_added"], 1)
                    dve.wait_ge(S["branch_added"], i + 1)
                    dve.sem_inc(S["piece_out"], 1)
                elif kind == "w_out2":
                    n = args[0]
                    dve.wait_ge(*piece_done(st))
                    v.scalar_tensor_tensor(out=h[:, n, :], in0=bank(p % 2), scalar=mod_v[:, 16 + n, 0:1], in1=h[:, n, :],
                                           op0=ALU.mult, op1=ALU.add).then_inc(S["x_res"], 1)
                    dve.wait_ge(S["x_res"], n + 1)
                    dve.sem_inc(S["piece_out"], 1)

            def walk(steps):
                for st in steps:
                    name = st[0]
                    if name == "piece":
                        piece(st)
                    elif name == "attn":
                        pv, tr, qk = (TILES[i] if i is not None else None for i in st[1:])
                        if qk:
                            for sub in range(qk.n_soft):
                                shift(qk, sub)
                        if tr:
                            move_pt(tr)
                        if qk:
                            for sub in range(qk.n_soft):
                                weigh(qk, sub)
                    elif name == "hg_front":
                        hd = st[1]
                        dve.wait_ge(S["piece_out"], piece_count("hg_og", (hd,)))
                        link(v.tensor_scalar(hg_sg, hg_sg, omlb[:, hd:hd + 1], lb[:, hd:hd + 1], ALU.mult, ALU.add))
                        v.tensor_scalar(hg_k, hg_sg, -1.0, 1.0, ALU.mult, ALU.add).then_inc(S["hg_f_done"], 1)
                        dve.wait_ge(S["hg_ln_done"], hd + 1)
                        link(v.tensor_tensor_scan(hg_sg, scan_keep, hg_b, 0.0, ALU.mult, ALU.add))
                        bv = hg_sg.rearrange("p (n c) -> p n c", c=64)
                        link(v.tensor_tensor(hg_t.rearrange("p (n c) -> p n c", c=64), bv,
                                             bv[:, :, 31:32].to_broadcast([P, 8, 64]), ALU.subtract))
                        v.tensor_tensor(hg_t2.rearrange("p (n c) -> p n c", c=64), bv,
                                        bv[:, :, 63:64].to_broadcast([P, 8, 64]), ALU.subtract
                                        ).then_inc(S["hg_shifted"], 1)
                        dve.wait_ge(S["hg_exps"], 5 * hd + 1)
                        v.tensor_tensor(hg_qe, hg_qe, hg_q, ALU.mult).then_inc(S["hg_queries"], 1)
                        dve.wait_ge(S["hg_exps"], 5 * hd + 3)
                        v.tensor_tensor(hg_kl, hg_kl, hg_k, ALU.mult).then_inc(S["hg_keys"], 1)
                        v.tensor_tensor(hg_ke, hg_ke, hg_k, ALU.mult).then_inc(S["hg_keys"], 1)
                        dve.wait_ge(S["hg_exps"], 5 * hd + 4)
                        v.tensor_tensor(hg_qb, hg_qb, hg_q, ALU.mult).then_inc(S["hg_queries"], 1)
                    elif name == "hg_scores":
                        hd = st[1]
                        dve.wait_ge(S["hg_score_mm"], hd + 1)
                        v.copy_predicated(hg_sc, hgmask[:], bank(2)).then_inc(S["hg_scored"], 1)
                    elif name == "hg_kv":
                        hd = st[1]
                        dve.wait_ge(S["hg_kv_mm"], hd + 1)
                        dve.wait_ge(S["hg_exps"], 5 * hd + 5)
                        link(v.tensor_copy(hg_state[:, 0, :], bank(3, 0, P)))
                        for n in range(1, 7):
                            ins = v.scalar_tensor_tensor(out=hg_state[:, n, :], in0=hg_state[:, n - 1, :],
                                                         scalar=hg_dec[:, n:n + 1],
                                                         in1=bank(3 + 2 * (n % 2), (n // 2) * P, P), op0=ALU.mult,
                                                         op1=ALU.add)
                            if n < 6:
                                link(ins)
                            else:
                                ins.then_inc(S["hg_states"], 1)
                    elif name == "hg_norm":
                        hd = st[1]
                        dve.wait_ge(S["hg_root"], hd + 1)
                        link(v.reciprocal(rinv[:], rms[:]))
                        link(v.scalar_tensor_tensor(out=hg_qe, in0=bank(6), scalar=col("hg_norm"), in1=rinv[:],
                                                    op0=ALU.mult, op1=ALU.mult))
                        v.tensor_tensor(yb[:, hd, :], hg_qe, hg_og, ALU.mult).then_inc(S["hg_done"], 1)
                    elif name == "rope":
                        r = rope_index(st)
                        tab = 0 if st[1] in ("ka", "qa") else 2
                        dst = {"ka": ka[:, N_CTX:768], "qa": qa[:, st[2], :], "kc": kc[:, min(st[2], 1), N_CTX:768],
                               "qc": qc[:, min(st[2], 1), :]}[st[1]]
                        dve.wait_ge(S["swap_mm"], r + 1)
                        link(v.tensor_tensor(rot, bank(7), rope[:, tab + 1, :], ALU.mult))
                        link(v.tensor_tensor(dst, raw[:, r % 2, 0:SEQ], rope[:, tab, :], ALU.mult))
                        v.tensor_tensor(dst, dst, rot, ALU.add).then_inc(S["roped"], 1)
                        dve.wait_ge(S["roped"], r + 1)
                    elif name == "diff_norm":
                        c = st[1]
                        dve.wait_ge(S["diff_root"], c + 1)
                        link(v.reciprocal(rinv[:], rms[:]))
                        link(v.scalar_tensor_tensor(out=rot, in0=bank(6), scalar=col("g_sub"), in1=rinv[:],
                                                    op0=ALU.mult, op1=ALU.mult))
                        v.tensor_scalar(yb[:, 6 + c, :], rot, 1.0 - LAM_INIT, None, ALU.mult).then_inc(S["o_out"], 1)
                    elif name == "gmlp_norm":
                        dve.wait_ge(S["turned"], turn_count("b_v", (1,)))
                        vf4 = vf.rearrange("p t (g d) -> p (t g) d", d=64)
                        vn4 = vn.rearrange("p t (g d) -> p (t g) d", d=64)
                        link(v.tensor_reduce(gm_mean, vf4, AX, ALU.add))
                        link(v.tensor_scalar(gm_mean, gm_mean, 1.0 / 64, None, ALU.mult))
                        link(v.tensor_tensor(vf4, vf4, gm_mean.rearrange("p (a b) -> p a b", b=1).to_broadcast([P, 16, 64]), ALU.subtract))
                        link(v.tensor_tensor(vn4, vf4, vf4, ALU.mult))
                        v.tensor_reduce(gm_var, vn4, AX, ALU.add).then_inc(S["gelu_norm_in"], 1)
                        dve.wait_ge(S["gelu_root"], 1)
                        link(v.reciprocal(gm_r, gm_var))
                        link(v.tensor_tensor(vf4, vf4, gm_r.rearrange("p (a b) -> p a b", b=1).to_broadcast([P, 16, 64]), ALU.mult))
                        for t in range(4):
                            ins = v.tensor_tensor(vn[:, t, :], vf[:, t, :], gtok, ALU.mult)
                        ins.then_inc(S["gelu_normed"], 1)
                    elif name == "gmlp":
                        c = st[1]
                        dve.wait_ge(S["gmlp_mm"], c + 1)
                        dve.wait_ge(S["piece_out"], piece_count("b_u", (c,)))
                        for t in range(4):
                            ins = v.tensor_tensor(rot[:, t * P:(t + 1) * P], bank(7, t * P, P), bsb[:, c, :], ALU.add)
                        link(ins)
                        v.tensor_tensor(yb[:, 4 + c, :], rot, ub[:, c, :], ALU.mult).then_inc(S["gmlp_done"], 1)

            walk(MIX1)
            invert(4, SEQ)
            add_normed("mix_post", lambda k: w_out_y[:, k, :], 1.0, 4)
            dve.wait_ge(S["h_done"], N_H[4])
            invert(5, SEQ)
            normalise_split(2, lambda k: h[:, k, :], lambda k: col("ffn2_pre", k))

            def ada_products(n, slot, ready, with_ctx):
                dve.wait_ge(landed[slot], ready)
                if with_ctx:
                    dve.wait_ge(S["ctx_summed"], n + 1)
                    v.tensor_tensor(ada_prod[:, 1, :], ring[:, slot, :], c_rows[:, 1, :], ALU.mult
                                    ).then_inc(S["ada_ctx"], 1)
                dve.wait_ge(S["x_summed"], n + 1)
                v.tensor_tensor(ada_prod[:, 0, :], ring[:, slot, :], c_rows[:, 0, :], ALU.mult).then_inc(S["ada_x"], 1)

            v.memset(mod, 0.0).then_inc(S["prep_dve"], 1)
            dve.wait_ge(S["prep_dve"], 4)
            dve.wait_ge(S["c_silu"], 1)
            for lo, hi in ((0, N_ADA_CTX // 4), (N_ADA_CTX // 4, NF // 2)):
                with dve.Fori(lo, hi) as i:
                    for q in range(2):
                        for w in range(2):
                            b = B_GU2 + 2 * w
                            ada_products(4 * i + 2 * q + w, b % SLOTS, 16 * (b // SLOTS + 1) + 16 * (2 * i + q), lo == 0)
                        hidden(1, 2 * i + q, q)
            for b in range(B_ADA_REST, B_DN2):
                ada_products(index_of(b), b % SLOTS, 16 * (b // SLOTS + 1), False)
            dve.wait_ge(S["x_summed"], 48 + 1)
            dve.wait_ge(S["ctx_summed"], N_ADA_CTX + 1)
            link(v.tensor_tensor(mod_v, mod_v,
                                 col("b_ada", 0, 48).rearrange("p (n c) -> p n c", c=1).to_broadcast([P, 48, 2]), ALU.add))
            for i, (sc_at, which, name) in enumerate(((8, 0, "g_mix"), (8, 1, "g_mix"), (32, 0, "g_ffn"))):
                g = gain[:, 8 * i:8 * i + 8]
                link(v.tensor_scalar(g, mod_v[:, sc_at:sc_at + 8, which], 1.0, None, ALU.add))
                link(v.tensor_tensor(g, g, col(name, 0, 8), ALU.mult))
            ffn_out(1, 6, "ffn2_post")
            dve.wait_ge(S["h_done"], N_H[6])
            invert(7, N_CTX)
            normalise_context(ctx_hi, ctx_lo, lambda k: ctx_raw[:, k, :], lambda k: gain[:, 8 + k:9 + k], N_CTX,
                              lambda k: mod_v[:, k, 1:2])
            dve.wait_ge(S["normed"], N_NORM_U[7])
            invert(8, SEQ)
            normalise_split(3, lambda k: h[:, k, :], lambda k: gain[:, k:k + 1], lambda k: mod_v[:, k, 0:1])
            dve.wait_ge(S["tables2"], 80)
            walk(MIX2)
            invert(9, SEQ)
            normalise(lambda k: u[:, k, :], lambda k: h[:, k, :], lambda k: gain[:, 16 + k:17 + k], SEQ,
                      lambda k: mod_v[:, 24 + k, 0:1])

            def r3(a, n, m):
                return rt[:, a:a + n * m].rearrange("p (t g) -> p t g", g=m)

            placed, lg, le, t16 = r3(0, 4, 16), r3(100, 4, 4), r3(116, 4, 16), r3(220, 4, 16)
            ge, tg, oh, f1, f2, leg, w4 = r3(80, 4, 4), r3(300, 4, 4), r3(184, 4, 4), r3(316, 4, 4), r3(332, 4, 4), r3(348, 4, 4), r3(364, 4, 4)
            e2 = rt[:, 200:204]
            m1, m2, ptop, w1, w2 = (rt[:, 204 + 0:208], rt[:, 208:212], rt[:, 212:216], rt[:, 64:68], rt[:, 68:72])
            order = const("first").rearrange("p (t g) -> p t g", g=4)

            def b3(x, m):
                return x.rearrange("p (t o) -> p t o", o=1).to_broadcast([P, 4, m])

            def first_of_max(dst, x, top):
                link(v.tensor_reduce(top, x, AX, ALU.max))
                link(v.tensor_tensor(tg, x, b3(top, 4), ALU.is_equal))
                link(v.tensor_tensor(tg, tg, order, ALU.mult))
                link(v.tensor_reduce(w1, tg, AX, ALU.max))
                link(v.tensor_tensor(dst, tg, b3(w1, 4), ALU.is_equal))

            dve.wait_ge(S["route_mm"], 1)
            logits = bank(7, 0, 128).rearrange("p (t g) -> p t g", g=32)
            bias = col("b_router", 0, 20).rearrange("p (o g) -> p o g", o=1)
            link(v.tensor_tensor(lg, logits[:, :, 0:4], bias[:, :, 0:4].to_broadcast([P, 4, 4]), ALU.add))
            link(v.tensor_tensor(le, logits[:, :, 4:20], bias[:, :, 4:20].to_broadcast([P, 4, 16]), ALU.add))
            first_of_max(oh, lg, m1)
            v.tensor_tensor(ge, lg, b3(m1, 4), ALU.subtract).then_inc(S["route_exp_in"], 1)
            dve.wait_ge(S["route_exp"], 1)
            link(v.tensor_reduce(ptop, ge, AX, ALU.add))
            link(v.reciprocal(ptop, ptop))
            for g in range(4):
                ins = v.tensor_tensor(t16[:, :, 4 * g:4 * g + 4], le[:, :, 4 * g:4 * g + 4],
                                      oh[:, :, g:g + 1].to_broadcast([P, 4, 4]), ALU.mult)
                link(ins)
            link(v.tensor_tensor(leg, t16[:, :, 0:4], t16[:, :, 4:8], ALU.add))
            link(v.tensor_tensor(leg, leg, t16[:, :, 8:12], ALU.add))
            link(v.tensor_tensor(leg, leg, t16[:, :, 12:16], ALU.add))
            first_of_max(f1, leg, m1)
            link(v.scalar_tensor_tensor(out=leg, in0=f1, scalar=-3.0e38, in1=leg, op0=ALU.mult, op1=ALU.add))
            first_of_max(f2, leg, m2)
            v.tensor_tensor(e2, m2, m1, ALU.subtract).then_inc(S["route_e2_in"], 1)
            dve.wait_ge(S["route_exp"], 2)
            link(v.tensor_scalar(w1, e2, 1.0, None, ALU.add))
            link(v.reciprocal(w1, w1))
            link(v.tensor_tensor(w1, w1, ptop, ALU.mult))
            link(v.tensor_tensor(w2, w1, e2, ALU.mult))
            link(v.tensor_tensor(leg, f1, f2, ALU.add))
            link(v.tensor_tensor(f1, f1, b3(w1, 4), ALU.mult))
            link(v.tensor_tensor(f2, f2, b3(w2, 4), ALU.mult))
            link(v.tensor_tensor(w4, f1, f2, ALU.add))
            gates = gates_e.rearrange("p e t -> p t e")
            for g in range(4):
                of_group = oh[:, :, g:g + 1].to_broadcast([P, 4, 4])
                link(v.tensor_tensor(routed[:, :, 4 * g:4 * g + 4], leg, of_group, ALU.mult))
                link(v.tensor_tensor(gates[:, :, 4 * g:4 * g + 4], w4, of_group, ALU.mult))
            dve.sem_inc(S["route_done"], 1)

            for i in range(8):
                part = slice((i % 2) * SEQ, (i % 2 + 1) * SEQ)
                dve.wait_ge(S["u_hi_done"], i + 1)
                v.tensor_tensor(t_lo[:, i // 2, part], bank(i % 4), t_hi[:, i // 2, part].bitcast(F32), ALU.subtract
                                ).then_inc(S["u_split"], 1)

            dve.wait_ge(S["place_mm"], 1)
            link(v.tensor_scalar(placed, bank(5, 0, 64).rearrange("p (t e) -> p t e", e=N_EXP), BIG, None, ALU.add))
            link(v.tensor_tensor(placed, placed, routed, ALU.mult))
            link(v.tensor_scalar(place[:, 0:N_EXP, :].rearrange("p e t -> p t e"), placed, -BIG, None, ALU.add))
            link(v.tensor_scalar(place[:, N_EXP:, :], place[:, 0:GROUP, :], -float(P), None, ALU.add))

            def build(first):
                for q in range(GROUP):
                    for t in range(4):
                        ins = v.tensor_scalar(sel[:, q, t, :], const("slot"), place[:, bass.ds(first + q, 1), t], None,
                                              ALU.is_equal)
                ins.then_inc(S["sel_done"], 1)

            build(0)
            dve.wait_ge(S["count_mm"], 1)
            most, more = rt[:, 64:65], rt[:, 65:68]
            link(v.tensor_reduce(most, bank(4, 0, N_EXP), AX, ALU.max))
            for k in range(3):
                link(v.tensor_scalar(more[:, k:k + 1], most, float((k + 1) * P), None, ALU.is_gt))
            link(v.tensor_reduce(most, more, AX, ALU.add))
            link(v.tensor_scalar(most, most, 1.0, None, ALU.add))
            v.tensor_copy(rounds_i[:], most).then_inc(S["rounds_known"], 1)

            dve.sem_inc(S["he_done"], 1)
            dve.sem_inc(S["y_lo_done"], 2)
            dve.sem_inc(S["back_added"], 1)
            dve.wait_ge(S["rounds_known"], 1)
            rounds = dve.alloc_register("rounds")
            dve.reg_load(rounds, rounds_i[0:1, 0:1])
            with dve.Fori(0, rounds) as r:
                with dve.Fori(0, N_EXP // GROUP) as g:
                    G = 4 * r + g

                    def add_back(q, lo, hi):
                        for c in range(lo, hi):
                            dve.wait_ge(S["back_mm"], 32 * G + 8 * q + c + 2)
                            v.scalar_tensor_tensor(out=h[:, c, :], in0=bank(5 + c % 2), scalar=mod_v[:, 40 + c, 0:1],
                                                   in1=h[:, c, :], op0=ALU.mult, op1=ALU.add
                                                   ).then_inc(S["back_added"], 1)

                    dve.wait_ge(S["gsel_mm"], G + 1)
                    v.tensor_copy(gsel, bank(2, 0, GROUP)).then_inc(S["gsel_out"], 1)
                    dve.wait_ge(S["gsel_out"], G + 1)
                    for q in range(GROUP):
                        if q:
                            add_back(q - 1, 0, EARLY)
                        dve.wait_ge(S["raw_used"], index_of(B_MOE) + 12 * q + 8 + 192 * r + 48 * g)
                        dve.wait_ge(S["silu_e"], 4 * G + q + 1)
                        dve.wait_ge(S["he_turned"], 4 * G + q + 1)
                        v.scalar_tensor_tensor(out=he, in0=moe_silu, scalar=gsel[:, q:q + 1], in1=bank(1), op0=ALU.mult,
                                               op1=ALU.mult).then_inc(S["he_done"], 1)
                        if q:
                            add_back(q - 1, EARLY, KC)
                        if q == 1:
                            dve.wait_ge(S["sel_used"], G + 2)
                            build(4 * g + GROUP)
                        for half in range(2):
                            part = slice(half * SEQ, (half + 1) * SEQ)
                            dve.wait_ge(S["y_hi_done"], 8 * G + 2 * q + half + 1)
                            v.tensor_tensor(y_lo[:, part], bank(3 + half), y_hi[:, part].bitcast(F32), ALU.subtract
                                            ).then_inc(S["y_lo_done"], 1)
                    add_back(GROUP - 1, 0, KC)
                v.tensor_scalar(place, place, -float(P), None, ALU.add).then_inc(S["place_shifted"], 1)
                dve.wait_ge(S["place_shifted"], r + 1)
                dve.wait_ge(S["back_added"], 128 * r + 129)
            dve.sem_inc(S["x_res"], KC)
            invert(10, SEQ)
            normalise(lambda k: u[:, k, :], lambda k: h[:, k, :], lambda k: col("g_final", k), SEQ)


PIECES = {(st[3], st[4]): st[1] for st in MIX1 + MIX2 if st[0] == "piece"}


def piece_count(kind, args):
    return PIECES[(kind, args)] + 1


TURNS = [st for st in MIX1 + MIX2 if st[0] == "turn"]


def turn_count(kind, args):
    return 1 + next(st[1] for st in TURNS if st[3:] == (kind, args))


def half_count(p):
    return sum(1 for st in MIX1 + MIX2 if st[0] == "piece" and not st[5] and st[1] <= p)


FIRST_U_PIECE = (PIECES[("mem_q", (0,))], PIECES[("a_k", ("x",))])

ROPES = [st for st in MIX2 if st[0] == "rope"]
ROPES.sort(key=lambda st: PIECES[{"ka": ("a_k", ("x",)), "qa": ("a_q", (st[2],)), "kc": ("c_k", (st[2], "x")),
                                  "qc": ("c_q", (st[2],))}[st[1]]])
assert [st for st in MIX2 if st[0] == "rope"] == ROPES


def rope_index(st):
    return ROPES.index(tuple(st))


def _bank7():
    table, last = {}, ("root_done", 4)
    for st in MIX1 + MIX2:
        after = {"hg_norm": lambda: ("hg_root", st[1] + 1), "rope": lambda: ("roped", rope_index(st) + 1),
                 "diff_norm": lambda: ("diff_root", st[1] + 1), "turn": lambda: ("turned", st[1] + 1),
                 "gmlp": lambda: ("gmlp_done", st[1] + 1)}.get(st[0])
        if after:
            table[st] = last
            last = after()
    return table


BANK7_READ = _bank7()


def last_c_tile(c):
    return max(t.index for t in TILES if t.kind == "c" and t.head // 2 == c)


def a_head(t):
    return t.head // 2 + 4 * (t.head % 2)


def branch_index(args):
    return ("mem", "hg", "dil").index(args[0]) * KC + args[1]


def _act_links():
    n, raws, sinks = 0, {}, {}
    for st in MIX2:
        if st[0] == "piece" and (st[3] in ("a_q", "c_q") or (st[3] in ("a_k", "c_k") and st[4][-1] == "x")):
            n += 1
            raws[{"a_k": "ka", "a_q": "qa", "c_k": "kc", "c_q": "qc"}[st[3]], 0 if st[3] == "a_k" else st[4][0]] = n
        if st[0] == "attn" and st[3] is not None and TILES[st[3]].kind == "a":
            n += 1
            sinks[st[3]] = n
    return raws, sinks


RAWS, N_ROPE_RAW_BEFORE_A = _act_links()


def raw_count(st):
    return RAWS[st[1], st[2]]


def _before(st, of):
    n = 0
    for x in MIX1:
        if x == st:
            return n
        if x[0] == "attn":
            n += of(x)
    raise KeyError(st)


def n_turned(st):
    return _before(st, lambda x: x[2] is not None)


def n_scored(st):
    return _before(st, lambda x: x[3] is not None)


def n_groups(st):
    return _before(st, lambda x: x[1] is not None and TILES[x[1]].last)


def columns(w):
    k, n = w.shape
    return w.reshape(k // P, P, n // P, P).transpose(2, 1, 0, 3).reshape(n // P, P, k)


def pairs(w):
    return w.reshape(4, P, 4, 2, P).transpose(2, 1, 3, 0, 4).reshape(4, P, 1024)


def feature_major(x):
    return np.ascontiguousarray(x.reshape(x.shape[0], -1, P).transpose(2, 1, 0))


def chunks(x):
    return x.reshape(-1, P).T


def stream_of(i):
    w_in, kv = columns(i["w_in"][0]), columns(i["w_mem_kv"][0])
    gu1, gu2 = columns(i["ffn1_w_gu"][0]), columns(i["ffn2_w_gu"][0])
    ada = i["w_ada_2"][0].T.reshape(48, P, D)
    blocks = []
    for f in range(NF):
        blocks += [gu1[f], gu1[NF + f]]
    blocks += list(i["ffn1_w_down"][0].reshape(NF, P, D))
    br = {"hg": pairs(i["w_br_hg"][0]), "dil": pairs(i["w_br_dil"][0]), "mem": pairs(i["w_br_mem"][0])}
    w_out = columns(i["w_out"][0])
    for st in MIX1:
        if st[0] != "piece" or not st[5]:
            continue
        kind, a = st[3], st[4]
        if kind == "mem_k":
            b = kv[a[0]]
        elif kind == "mem_v":
            b = kv[4 + a[0]]
        elif kind == "mem_q":
            b = w_in[52 + a[0]]
        elif kind[:3] == "hg_":
            b = w_in[{"hg_q": 0, "hg_f": 4, "hg_v": 8, "hg_og": 12}[kind] + a[0]]
        elif kind[:4] == "dil_":
            b = w_in[16 + (a[1] * 3 + "qkv".index(kind[4])) * 4 + a[0]]
        elif kind == "gate":
            b = w_in[56 + {"hg": 0, "dil": 8, "mem": 16}[a[0]] + a[1]]
        elif kind == "branch":
            b = br[a[0]][a[1] // 2]
        else:
            b = w_out[a[0]]
        blocks.append(b)
    for f in range(NF):
        blocks += [ada[2 * f], gu2[f], ada[2 * f + 1], gu2[NF + f]]
    blocks += [ada[44 + n] for n in range(4)]
    blocks += list(i["ffn2_w_down"][0].reshape(NF, P, D))
    w2 = i["w_in_2"][0]
    order = [c for j in range(4) for hd in (j, j + 4) for c in range(hd * 64, hd * 64 + 64)]
    a_q, rest = columns(w2[:, order]), columns(w2[:, 512:])
    wo2 = i["w_out_2"][0]
    w_out2 = columns(np.concatenate([wo2[order], wo2[512:]], axis=0))
    for st in MIX2:
        if st[0] != "piece" or not st[5]:
            continue
        kind, a = st[3], st[4]
        b = {"a_q": lambda: a_q[a[0]], "a_k": lambda: rest[0], "a_v": lambda: rest[1], "b_u": lambda: rest[2 + a[0]],
             "b_v": lambda: rest[4 + a[0]], "c_q": lambda: rest[6 + a[0]], "c_k": lambda: rest[8 + a[0]],
             "c_v": lambda: rest[10 + a[0]], "w_out2": lambda: w_out2[a[0]]}[kind]()
        blocks.append(b)
    for e in range(N_EXP):
        g, up = (i[name][0, e].reshape(4, 2, P, D_EXP).transpose(0, 2, 1, 3).reshape(4, P, 1024)
                 for name in ("w_gate_2", "w_up_2"))
        for k in range(4):
            blocks += [g[k], up[k]]
        blocks += list(i["w_down_2"][0, e].reshape(4, P, D))
    assert len(blocks) == N_BLOCKS
    return np.stack(blocks)


def shape_constants():
    p = np.arange(P)
    eye = np.eye(P)
    window = np.zeros((P, 384))
    d = p[:, None] + P - np.arange(384)[None, :]
    window[np.abs(d) > P] = -1e30
    parts = {"ident": eye, "mean_d": np.full((P, P), 1.0 / D), "ones": np.ones((P, P)),
             "mean_128": np.full((P, P), 1.0 / P), "mean_64": (p[:, None] // 64 == p[None, :] // 64) / 64.0,
             "swap16": eye[p ^ 16], "swap8": eye[p ^ 8], "window": window,
             "before": p[:, None] < p[None, :], "slot": np.broadcast_to(p, (P, P)),
             "first": np.broadcast_to(np.tile([4.0, 3.0, 2.0, 1.0], 4), (P, 16))}
    consts = np.concatenate([parts[n] for n in CONSTS], axis=1).astype(np.float32)
    keep = np.broadcast_to((np.arange(SEQ) % 64 != 0), (P, SEQ)).astype(np.float32)
    same = (p[:, None] // 64 == p[None, :] // 64) & (p[:, None] <= p[None, :])
    hgmask = np.tile(same, (1, 4)).astype(np.uint32)
    dist = np.full((P, 4, 768), 1e30)
    lk = np.arange(P)
    for r in range(4):
        tq = 4 * p + r
        for kr in range(4):
            dd = tq[:, None] - (4 * lk + kr)[None, :]
            dist[:, r, kr * P:(kr + 1) * P] = np.where((dd >= 0) & (dd <= 128), dd, 1e30)
        dd = tq[:, None] - (4 * lk + r)[None, :]
        dist[:, r, 512:640] = np.where(dd >= 0, dd, 1e30)
        dist[:, r, 640:768] = np.where((dd >= 0) & (dd % 16 == 0), dd, 1e30)
    rope = np.zeros((P, 4, SEQ), np.float32)
    t = np.arange(SEQ)
    for at, dh in ((0, 64), (2, 32)):
        n = dh // 4
        inv = (np.float32(10000.0) ** (-np.arange(n, dtype=np.float32) / np.float32(n))).astype(np.float32)
        dd = p % dh
        pos = np.where((dd < dh // 2)[:, None], (t // 64)[None, :], (t % 64)[None, :]).astype(np.float32)
        ang = (pos * inv[dd % n][:, None]).astype(np.float32).astype(np.float64)
        sign = np.where((dd // n) % 2 == 0, -1.0, 1.0)[:, None]
        rope[:, at] = np.cos(ang)
        rope[:, at + 1] = np.sin(ang) * sign
    return consts, keep, hgmask, dist.astype(np.float32), rope


def kernel(**inputs):
    import concourse.bacc as bacc
    from concourse.bass_utils import run_bass_kernel_spmd

    i = {k: np.asarray(v) for k, v in inputs.items()}
    f32 = np.float32
    cols = np.zeros((P, N_COLS), f32)
    for name, key in (("ffn1_pre", "ffn1_pre_w"), ("ffn1_post", "ffn1_post_w"), ("mix_pre", "mix_pre_w"),
                      ("mix_post", "mix_post_w"), ("ffn2_pre", "ffn2_pre_w"), ("ffn2_post", "ffn2_post_w"),
                      ("mem_norm", "mem_norm_w"), ("g_mix", "g_mix_2"), ("g_ffn", "g_ffn_2"), ("g_final", "g_final_2"),
                      ("b_gate", "b_gate"), ("b_ada", "b_ada_2"), ("hg_norm", "hg_norm_w")):
        cols[:, slice(*COLS[name])] = chunks(i[key].reshape(-1))
    cols[:, slice(*COLS["hg_lb0"])] = chunks(i["hg_lb_logits"][0])
    cols[:, slice(*COLS["hg_lb1"])] = chunks(i["hg_lb_logits"][1])
    cols[:, COLS["g_sub"][0]] = np.tile(i["g_sub_2"][0], 2)
    cols[:, slice(*COLS["sink"])] = i["sink_2"]
    for k, key in enumerate(("lam_q1_2", "lam_q2_2", "lam_k1_2", "lam_k2_2")):
        cols[0:32, COLS["lam"][0] + k] = i[key][0]
    cols[:, slice(*COLS["b_router"])] = np.concatenate([i["b_rg_2"], i["b_re_2"]], axis=1)
    consts, keep, hgmask, dist, rope = shape_constants()
    router = np.concatenate([i["w_rg_2"][0], i["w_re_2"][0]], axis=1).reshape(KC, P, 20).transpose(1, 0, 2)
    bs = i["bs_tok_2"][0]
    arrays = {
        "stream": stream_of(i),
        "x_t": feature_major(i["x"][0]), "mem_t": feature_major(i["mem"][0]), "ctx_t": feature_major(i["ctx_2"][0]),
        "c_rows": np.broadcast_to(np.stack([i["c_2"][0], i["c_ctx_2"]]), (P, 2, D)),
        "cols": cols, "consts": consts, "keep": keep, "hgmask": hgmask, "dist": dist, "rope": rope,
        "gtok": np.broadcast_to(i["g_tok_2"][0].reshape(1, 256), (P, 256)),
        "bs": np.repeat(bs, 64, axis=0).reshape(2, P, P).transpose(1, 0, 2),
        "ws": i["ws_tok_2"][0].transpose(2, 0, 1), "router": router,
    }
    arrays = {f"in_{k}": np.ascontiguousarray(a) for k, a in arrays.items()}
    nc = bacc.Bacc("TRN2", target_bir_lowering=False, num_devices=1, dynamic_dma_scratch_size=1024)
    args = [nc.dram_tensor(k, a.shape, mybir.dt.from_np(a.dtype), kind="ExternalInput").ap() for k, a in arrays.items()]
    args.append(nc.dram_tensor("out_t", (P, KC, SEQ), F32, kind="ExternalOutput").ap())
    two_blocks_kernel(nc, *args)
    r = run_bass_kernel_spmd(nc, [arrays], core_ids=[0])
    got = r.results[0]["out_t"]
    return np.ascontiguousarray(got.transpose(2, 1, 0).reshape(1, SEQ, D))
```
